# Optimizing a Trainium2 kernel written in Bass

```python
import math
import jax, jax.numpy as jnp
from jax import lax
import numpy as np

D_MODEL = 1024
BATCH = 1
SEQ = 256
DEPTH = 2

N_MIXERS = 2
N_SUB = 3
D_FF = 2816
D_RNN = D_MODEL
RG_HEADS = 8
RG_HEAD_DIM = D_RNN // RG_HEADS
CONV_W = 4
RG_C = 8.0
D_G = 2 * D_MODEL
GM_GROUPS = 8
GM_GROUP_DIM = D_G // GM_GROUPS
CHUNK = 128
N_RG = (DEPTH + 1) // 2
N_GM = DEPTH // 2
EPS = 1e-6

kernel_name = "hybrid_rglru_gmlp_macaron_trunk"

def rmsnorm(x, g):
    xf = x.astype(jnp.float32)
    y = xf * lax.rsqrt(jnp.mean(xf * xf, axis=-1, keepdims=True) + EPS)
    return (y * g.astype(jnp.float32)).astype(x.dtype)

def layernorm(x, g, b):
    xf = x.astype(jnp.float32)
    mu = jnp.mean(xf, axis=-1, keepdims=True)
    var = jnp.mean(jnp.square(xf - mu), axis=-1, keepdims=True)
    y = (xf - mu) * lax.rsqrt(var + EPS)
    return (y * g.astype(jnp.float32) + b.astype(jnp.float32)).astype(x.dtype)

def swiglu(h, w_in, w_out):
    gate, up = jnp.split(h @ w_in, 2, axis=-1)
    return (jax.nn.silu(gate) * up) @ w_out

def causal_depthwise_conv(x, w, b):
    S = x.shape[1]
    xp = jnp.pad(x, ((0, 0), (CONV_W - 1, 0), (0, 0)))
    y = b
    for k in range(CONV_W):
        y = y + xp[:, k:k + S, :] * w[k]
    return y

def _lin_combine(left, right):
    a1, b1 = left
    a2, b2 = right
    return a1 * a2, a2 * b1 + b2

def rglru_mixer(h, w_in, conv_w, conv_b, w_a, b_a, w_x, b_x, lam, w_out):
    B, S, _ = h.shape
    xb, gb = jnp.split(h @ w_in, 2, axis=-1)
    xb = causal_depthwise_conv(xb, conv_w, conv_b)
    xh = xb.reshape(B, S, RG_HEADS, RG_HEAD_DIM)
    r = jax.nn.sigmoid(jnp.einsum('bshd,hde->bshe', xh, w_a).reshape(B, S, D_RNN) + b_a)
    i = jax.nn.sigmoid(jnp.einsum('bshd,hde->bshe', xh, w_x).reshape(B, S, D_RNN) + b_x)
    log_a = -RG_C * r.astype(jnp.float32) * jax.nn.softplus(-lam.astype(jnp.float32))
    a = jnp.exp(log_a)
    mult = jnp.sqrt(-jnp.expm1(2.0 * log_a))
    bt = mult * (i * xb).astype(jnp.float32)
    _, hs = lax.associative_scan(_lin_combine, (a, bt), axis=1)
    y = hs.astype(h.dtype) * jax.nn.gelu(gb)
    return y @ w_out

def gmlp_mixer(h, w_in, ln_g, ln_b, w_s, b_s, w_out):
    B, S, _ = h.shape
    u, v = jnp.split(jax.nn.gelu(h @ w_in), 2, axis=-1)
    v = layernorm(v, ln_g, ln_b)
    vc = v.reshape(B, S // CHUNK, CHUNK, GM_GROUPS, GM_GROUP_DIM)
    mask = jnp.tril(jnp.ones((CHUNK, CHUNK), dtype=w_s.dtype))
    ws = w_s * mask
    vm = jnp.einsum('gts,bcsgd->bctgd', ws, vc) + b_s.T[None, None, :, :, None]
    y = u * vm.reshape(B, S, D_G)
    return y @ w_out

def setup_inputs(seed: int = 0) -> dict:
    key = jax.random.key(seed)
    ks = jax.random.split(key, 32)
    nrm = lambda k, shape, s: jax.random.normal(k, shape, jnp.float32) * s
    D = D_MODEL
    u_lam = jax.random.uniform(ks[20], (N_RG, D_RNN), jnp.float32, 0.9, 0.999)
    return {
        "x": nrm(ks[0], (BATCH, SEQ, D), 1.0),
        "c": nrm(ks[1], (BATCH, D), 1.0),
        "ada_w": nrm(ks[2], (DEPTH, D, N_SUB * 3 * D), 0.5 * D ** -0.5),
        "ada_b": nrm(ks[3], (DEPTH, N_SUB * 3 * D), 0.01),
        "norm_pre": 1.0 + nrm(ks[4], (DEPTH, N_SUB, D), 0.05),
        "norm_post": 1.0 + nrm(ks[5], (DEPTH, N_SUB, D), 0.05),
        "ffn_w_in": nrm(ks[6], (DEPTH, 2, D, 2 * D_FF), D ** -0.5),
        "ffn_w_out": nrm(ks[7], (DEPTH, 2, D_FF, D), D_FF ** -0.5),
        "rg_w_in": nrm(ks[8], (N_RG, D, 2 * D_RNN), D ** -0.5),
        "rg_conv_w": nrm(ks[9], (N_RG, CONV_W, D_RNN), CONV_W ** -0.5),
        "rg_conv_b": nrm(ks[10], (N_RG, D_RNN), 0.01),
        "rg_w_a": nrm(ks[11], (N_RG, RG_HEADS, RG_HEAD_DIM, RG_HEAD_DIM), RG_HEAD_DIM ** -0.5),
        "rg_b_a": nrm(ks[12], (N_RG, D_RNN), 0.01),
        "rg_w_x": nrm(ks[13], (N_RG, RG_HEADS, RG_HEAD_DIM, RG_HEAD_DIM), RG_HEAD_DIM ** -0.5),
        "rg_b_x": nrm(ks[14], (N_RG, D_RNN), 0.01),
        "rg_lambda": jnp.log(u_lam) - jnp.log1p(-u_lam),
        "rg_w_out": nrm(ks[15], (N_RG, D_RNN, D), D_RNN ** -0.5),
        "gm_w_in": nrm(ks[16], (N_GM, D, 2 * D_G), D ** -0.5),
        "gm_ln_g": 1.0 + nrm(ks[17], (N_GM, D_G), 0.05),
        "gm_ln_b": nrm(ks[18], (N_GM, D_G), 0.01),
        "gm_w_s": nrm(ks[19], (N_GM, GM_GROUPS, CHUNK, CHUNK), CHUNK ** -0.5),
        "gm_b_s": 1.0 + nrm(ks[21], (N_GM, GM_GROUPS, CHUNK), 0.1),
        "gm_w_out": nrm(ks[22], (N_GM, D_G, D), D_G ** -0.5),
    }

def reference(x, c, ada_w, ada_b, norm_pre, norm_post, ffn_w_in, ffn_w_out,
              rg_w_in, rg_conv_w, rg_conv_b, rg_w_a, rg_b_a, rg_w_x, rg_b_x,
              rg_lambda, rg_w_out, gm_w_in, gm_ln_g, gm_ln_b, gm_w_s, gm_b_s,
              gm_w_out):
    B = x.shape[0]
    c_act = jax.nn.silu(c)

    def sublayer(x, l, j, mod, fn, res_w):
        shift, scale, gate = mod[:, j, 0], mod[:, j, 1], mod[:, j, 2]
        h = rmsnorm(x, norm_pre[l, j]) * (1.0 + scale[:, None, :]) + shift[:, None, :]
        o = rmsnorm(fn(h), norm_post[l, j])
        return x + res_w * gate[:, None, :] * o

    for l in range(DEPTH):
        mod = (c_act @ ada_w[l] + ada_b[l]).reshape(B, N_SUB, 3, D_MODEL)
        x = sublayer(x, l, 0, mod, lambda h: swiglu(h, ffn_w_in[l, 0], ffn_w_out[l, 0]), 0.5)
        if l % N_MIXERS == 0:
            k = l // 2
            mix = lambda h: rglru_mixer(h, rg_w_in[k], rg_conv_w[k], rg_conv_b[k],
                                        rg_w_a[k], rg_b_a[k], rg_w_x[k], rg_b_x[k],
                                        rg_lambda[k], rg_w_out[k])
        else:
            k = l // 2
            mix = lambda h: gmlp_mixer(h, gm_w_in[k], gm_ln_g[k], gm_ln_b[k],
                                       gm_w_s[k], gm_b_s[k], gm_w_out[k])
        x = sublayer(x, l, 1, mod, mix, 1.0)
        x = sublayer(x, l, 2, mod, lambda h: swiglu(h, ffn_w_in[l, 1], ffn_w_out[l, 1]), 0.5)
    return x


_drawn_inputs = setup_inputs


def setup_inputs(seed=0):
    import zlib

    import numpy as np

    out = dict(_drawn_inputs(seed))
    spreads = {}
    factors = {'ada_b': 2.801,
     'rg_conv_b': 8.0,
     'rg_b_a': 64.0,
     'rg_b_x': 46.074,
     'gm_ln_g': 33.47,
     'gm_ln_b': 64.0,
     'gm_b_s': 7.932}
    for name, (base, spread) in spreads.items():
        noise = np.random.default_rng([zlib.crc32(name.encode()), seed]).standard_normal(out[name].shape)
        drawn = base * np.exp(spread * noise) if base else spread * noise
        out[name] = __import__('jax').numpy.asarray(drawn.astype(out[name].dtype))
    for name, factor in factors.items():
        out[name] = (out[name] * factor).astype(out[name].dtype)
    return out
```

```python
from contextlib import ExitStack

import concourse.bass as bass
from concourse import mybir

ALU = mybir.AluOpType
ACT = mybir.ActivationFunctionType
F32 = mybir.dt.float32
F32R = mybir.dt.float32r

P = 128
EPS = 1e-6


def trunk(nc, x, c, ada_w, ada_b, norm_pre, norm_post, ffn_w_in, ffn_w_out,
          rg_w_in, rg_conv_w, rg_conv_b, rg_w_a, rg_b_a, rg_w_x, rg_b_x,
          rg_lambda, rg_w_out, gm_w_in, gm_ln_g, gm_ln_b, gm_w_s, gm_b_s,
          gm_w_out, out):
    _, SEQ, D = x.shape
    TOKS = SEQ // P
    KD = D // P
    D_FF = ffn_w_out.shape[2]
    KF = D_FF // P
    HEADS, CONV = rg_w_a.shape[1], rg_conv_w.shape[1]
    D_G = gm_w_out.shape[1]
    GROUPS = gm_w_s.shape[1]
    GD = D_G // GROUPS
    DEPTH = ada_w.shape[0]
    N_SUB = 3
    NSUBL = DEPTH * N_SUB
    assert (TOKS, KD, KF % 2, CONV, HEADS, GROUPS, NSUBL) == (2, 8, 0, 4, KD, 8, 6)

    UNIT = 1024
    HALF = 512
    SLOTS = 4
    TURN_AT = 3
    ROUND = 4
    TAIL = 4

    subs = []
    units = in_rounds = silus = mixed = pairs = zpairs = 0
    for i in range(NSUBL):
        l, j = divmod(i, N_SUB)
        kind = "ffn" if j != 1 else ("rg" if l % 2 == 0 else "gm")
        kz = {"ffn": KF, "rg": KD, "gm": D_G // P}[kind]
        rounds = {"ffn": D_FF // (HALF // 2), "rg": 2 * D // HALF, "gm": 2 * D_G // HALF}[kind]
        n_pairs = {"ffn": KF // 2, "rg": KD, "gm": kz // 2}[kind]
        subs.append(dict(i=i, l=l, j=j, kind=kind, kz=kz, rounds=rounds, res=1.0 if j == 1 else 0.5,
                         ub=units, rb=in_rounds, sb=silus, mb=mixed, tb=pairs, zb=zpairs))
        units += rounds * ROUND + kz
        in_rounds += rounds
        silus += rounds if kind == "ffn" else 0
        mixed += 0 if kind == "ffn" else TOKS * rounds
        pairs += n_pairs
        zpairs += kz // 2
    RG, GM = subs[1], subs[4]

    def out_base(s):
        return s["ub"] + s["rounds"] * ROUND

    def y_bank(s, t):
        if t == 1:
            return 6
        return 2 if (s["rounds"] - 1) % 2 == 0 else 0

    def mod_bank(s):
        return 2 - y_bank(s, 0)

    ADA_IN = {"rg": {3: 0, 8: 1, 10: 2, 12: 3, 14: 4}, "gm": {3: 0, 7: 1, 11: 2, 15: 3, 23: 4, 27: 5}}
    ADA5_AT = {"rg": 0}
    ADA6_AT = {"ffn": 1, "rg": 2, "gm": 1}
    ADA7_AT = {"ffn": 7, "rg": 3, "gm": 7}
    MOD_AT = {"ffn": 13, "rg": 5, "gm": 11}

    ada_v = ada_w.rearrange("l (k p) (b c) -> l k b p c", p=P, c=D)
    adab_v = ada_b.rearrange("l (b c) -> l b c", c=D)
    ffn_in_v = ffn_w_in.rearrange("l s (p k) (g n c) -> l s n p (k g) c", p=P, g=2, c=HALF // 2)
    ffn_out_v = ffn_w_out.rearrange("l s (k p) n -> l s k p n", p=P)
    rg_in_v = rg_w_in.rearrange("l (p k) (n c) -> l n p k c", p=P, c=HALF)
    gm_in_v = gm_w_in.rearrange("l (p k) (n c) -> l n p k c", p=P, c=HALF)
    rg_out_v = rg_w_out.rearrange("l (k p) n -> l k p n", p=P)
    gm_out_v = gm_w_out.rearrange("l (k p) n -> l k p n", p=P)

    ROW_C = 0
    ROW_CW = ROW_C + KD
    ROW_CB = ROW_CW + CONV * KD
    ROW_BA, ROW_BX, ROW_LAM, ROW_BS = ROW_CB + KD, ROW_CB + 2 * KD, ROW_CB + 3 * KD, ROW_CB + 4 * KD
    ROWS = ROW_BS + GROUPS

    ctx = ExitStack()
    with ctx:
        def sb(name, shape, dt=F32):
            return ctx.enter_context(nc.sbuf_tensor(name, shape, dt))

        def sem(name):
            return ctx.enter_context(nc.semaphore(name))

        xres = sb("xres", [P, TOKS, D])
        h_hi = sb("h_hi", [P, KD, SEQ], F32R)
        h_lo = sb("h_lo", [P, KD, SEQ], F32R)
        z_hi = sb("z_hi", [P, KF, SEQ], F32R)
        z_lo = sb("z_lo", [P, KF, SEQ], F32R)
        w_raw = sb("w_raw", [P, SLOTS, UNIT])
        w_hi = sb("w_hi", [P, SLOTS, UNIT], F32R)
        w_lo = sb("w_lo", [P, SLOTS, UNIT], F32R)
        ada_raw = sb("ada_raw", [P, 3, D])
        ada_acc = sb("ada_acc", [P, 3, D])
        gate_sc = sb("gate_sc", [P, D])
        stage = sb("stage", [P, 2, TOKS, HALF])
        MIX = HEADS * (SEQ + CONV - 1) + 3 * HEADS * SEQ
        mix = sb("mix", [P, MIX])
        gate_w = sb("gate_w", [P, 2, HEADS, P])
        gate_t = sb("gate_t", [P, 4, SEQ])
        ws_t = sb("ws_t", [P, GROUPS, P])
        prm_rows = sb("prm_rows", [ROWS, P])
        pre_g = sb("pre_g", [P, NSUBL, KD])
        prm = sb("prm", [P, ROWS])
        ident = sb("ident", [P, P])
        ones = sb("ones", [P, P])
        c_act = sb("c_act", [P, KD, 1])
        mod_a = sb("mod_a", [P, KD])
        mod_b = sb("mod_b", [P, KD])
        sumsq = sb("sumsq", [P, 4])
        rms = sb("rms", [P, 4])
        msq = sb("msq", [P, 4])
        neg_half = sb("neg_half", [P, 1])
        bn = sb("bn", [P, TOKS, 4, 6])
        ln_mv = sb("ln_mv", [P, TOKS, 2])
        ln_ve = sb("ln_ve", [P, TOKS])
        ln_r = sb("ln_r", [P, TOKS])
        sp = sb("sp", [P, 9, KD])
        LAM_E, LAM_W, LAM_W2, LAM_Q, LAM_T, SP_P, SP_N, HBA, HBX = range(9)

        xb_pad = mix[:, 0:HEADS * (SEQ + CONV - 1)].rearrange("p (h t) -> p h t", h=HEADS)
        o0 = HEADS * (SEQ + CONV - 1)
        HS = HEADS * SEQ
        rg_m = mix[:, 0:HS].rearrange("p (h t) -> p h t", h=HEADS)
        rg_x = mix[:, o0:o0 + HS].rearrange("p (h t) -> p h t", h=HEADS)
        rg_a = mix[:, o0 + HS:o0 + 2 * HS].rearrange("p (h t) -> p h t", h=HEADS)
        rg_g = mix[:, o0 + 2 * HS:o0 + 3 * HS].rearrange("p (h t) -> p h t", h=HEADS)
        gm_v = mix[:, 0:TOKS * D_G].rearrange("p (t n) -> p t n", t=TOKS)
        gm_lg = mix[:, TOKS * D_G:(TOKS + 1) * D_G]
        gm_lb = mix[:, (TOKS + 1) * D_G:(TOKS + 2) * D_G]
        tmp2 = stage[:, 1, :, :]
        xn_stage = stage[:, 0, :, :].rearrange("p a b -> p (a b)")
        h_stage = stage[:, 1, :, :].rearrange("p a (k t) -> p (a k) t", t=P)
        junk = gate_t[:].rearrange("p (a b) t -> p a (b t)", a=2)
        LAND = 4
        land = mix[:, 0:LAND * 2 * D].rearrange("p (s q c) -> p s q c", s=LAND, q=2)

        def pair_of(z, n, it=0, per=0):
            return z[:].rearrange("p (n k) t -> p n k t", k=2)[:, it * per + n]

        ps = ctx.enter_context(nc.psum_tensor("ps", [P, 8, HALF], F32))

        raw_landed = [sem(f"raw_landed{n}") for n in range(SLOTS)]
        hi_done, lo_done = sem("hi_done"), sem("lo_done")
        unit_used = sem("unit_used")
        in_ready = sem("in_ready")
        silu_done, z_staged = sem("silu_done"), sem("z_staged")
        mix_staged = sem("mix_staged")
        u_staged = sem("u_staged")
        pair_done = sem("pair_done")
        zhi_done, z_ready = sem("zhi_done"), sem("z_ready")
        rg_pair_read = sem("rg_pair_read")
        y_ready = sem("y_ready")
        y_sq, y_rms, x_new = sem("y_sq"), sem("y_rms"), sem("x_new")
        y_scaled = sem("y_scaled")
        x_sq, x_rms, x_normed = sem("x_sq"), sem("x_rms"), sem("x_normed")
        x_turned, h_full, hhi_done, h_ready = (sem("x_turned"), sem("h_full"), sem("hhi_done"),
                                               sem("h_ready"))
        ada_landed = [sem(f"ada_landed{q}") for q in range(3)]
        ada_added = sem("ada_added")
        land_full = [sem(f"land_full{n}") for n in range(LAND)]
        land_added = sem("land_added")
        acc_zero, acc_bias = sem("acc_zero"), sem("acc_bias")
        mod_summed = sem("mod_summed")
        mod_set = sem("mod_set")
        post_landed = sem("post_landed")
        prm_landed, x_landed, ws_landed = sem("prm_landed"), sem("x_landed"), sem("ws_landed")
        pre_landed = sem("pre_landed")
        prm_turned, prm_done, c_done = sem("prm_turned"), sem("prm_done"), sem("c_done")
        lam_abs, lam_exp = sem("lam_abs"), sem("lam_exp")
        consts = sem("consts")
        pool_step = sem("pool_step")
        dve_step = sem("dve_step")
        act_step = sem("act_step")
        ws_turned, ws_copied, ws_masked = sem("ws_turned"), sem("ws_copied"), sem("ws_masked")
        gate_w_landed = sem("gate_w_landed")
        pads = sem("pads")
        conv_done, gates_done, gates_read = sem("conv_done"), sem("gates_done"), sem("gates_read")
        tan_done, exp_done = sem("tan_done"), sem("exp_done")
        m2_done, mult_done, hs_done = sem("m2_done"), sem("mult_done"), sem("hs_done")
        ln_landed, ln_var, ln_rstd, v_normed = (sem("ln_landed"), sem("ln_var"), sem("ln_rstd"),
                                                sem("v_normed"))
        sp_done, sp_read = sem("sp_done"), sem("sp_read")
        out_landed = sem("out_landed")

        block = ctx.enter_context(nc.Block())

        @block.sync
        def _(sync):
            def unit(u, src, n=0, runs=1):
                s = u % SLOTS
                if u >= SLOTS:
                    sync.wait_ge(lo_done, u - SLOTS + 1 + n)
                d = w_raw[:, s, :]
                if runs > 1:
                    d = d.rearrange("p (k c) -> p k c", k=runs)
                sync.dma_start(d, src).then_inc(raw_landed[s], 16)

            def ffn_round(s, r, it=0, per=0):
                v = ffn_in_v[s["l"], s["j"] // 2]
                for q in range(ROUND):
                    unit(s["ub"] + r * ROUND + q, v[it * per + r, :, 4 * q:4 * q + 4, :],
                         n=it * (per * ROUND), runs=4)

            def mixer_round(s, v, r, steps):
                col = r if s["kind"] == "rg" else (r + s["rounds"] // 2) % s["rounds"]
                for q in range(ROUND):
                    unit(s["ub"] + r * ROUND + q, v[col, :, 2 * q:2 * q + 2, :], runs=2)
                    if r * ROUND + q in steps:
                        ada(s["i"], steps[r * ROUND + q])

            def ada(i, k, it=0):
                l, j = divmod(i, N_SUB)
                l2, j2 = divmod(i + 1, N_SUB)
                blocks = [(l, 3 * j + 2)] + ([(l2, 3 * j2), (l2, 3 * j2 + 1)] if i + 1 < NSUBL else [])
                for q, (lq, b) in enumerate(blocks):
                    if k >= 1:
                        sync.wait_ge(ada_added, 3 * i * KD + len(blocks) * (k - 1) + q + 1 + it * len(blocks))
                    elif i >= 1:
                        sync.wait_ge(ada_added, 3 * (i * KD - 1) + q + 1)
                    sync.dma_start(ada_raw[:, q, :], ada_v[lq, it + k, b]).then_inc(ada_landed[q], 16)

            for k in range(KD):
                if k >= LAND:
                    sync.wait_ge(land_added, 2 * (k - LAND) + 2)
                for q in range(2):
                    sync.dma_start(land[:, k % LAND, q, :], ada_v[0, k, q]).then_inc(land_full[k % LAND], 16)
            ffn_round(subs[0], 0)

            for s in subs:
                i, kind = s["i"], s["kind"]
                if kind == "ffn":
                    if i > 0:
                        ffn_round(s, 0)
                    ada(i, 0)
                    with sync.Fori(0, (s["rounds"] - 1) // 2) as it:
                        ffn_round(s, 1, it, 2)
                        ada(i, 1, it)
                        ffn_round(s, 2, it, 2)
                else:
                    v = (rg_in_v if kind == "rg" else gm_in_v)[s["l"] // 2]
                    for r in range(s["rounds"]):
                        mixer_round(s, v, r, ADA_IN[kind])
                wv = {"ffn": ffn_out_v[s["l"], s["j"] // 2], "rg": rg_out_v[0], "gm": gm_out_v[0]}[kind]
                ob, o = out_base(s), 0

                def out_units(n):
                    if n >= 8:
                        with sync.Fori(0, n // 4) as it:
                            for q in range(4):
                                unit(ob + o + q, wv[it * 4 + (o + q)], n=it * 4)
                        for q in range(n // 4 * 4, n):
                            unit(ob + o + q, wv[o + q])
                    else:
                        for q in range(n):
                            unit(ob + o + q, wv[o + q])

                for at, k in ((ADA5_AT, 5), (ADA6_AT, 6), (ADA7_AT, 7)):
                    if kind in at:
                        out_units(at[kind] + 1 - o)
                        o = at[kind] + 1
                        ada(i, k)
                out_units(s["kz"] - o)

            for t in range(TOKS):
                sync.wait_ge(x_new, 2 * (NSUBL - 1) + t + 1)
                sync.dma_start(out[0, t * P:(t + 1) * P, :], xres[:, t, :]).then_inc(out_landed, 16)
            sync.wait_ge(out_landed, 16 * TOKS)

        @block.gpsimd
        def _(pool):
            steps = [0]

            def link(ins):
                steps[0] += 1
                ins.then_inc(pool_step, 1)
                pool.wait_ge(pool_step, steps[0])

            def acc_init(m):
                lo, hi = (1, 3) if m == 0 else ((0, 1) if m == NSUBL else (0, 3))
                if m >= 1:
                    pool.wait_ge(mod_summed, m)
                nc.gpsimd.memset(ada_acc[:, lo:hi, :], 0.0).then_inc(acc_zero, 1)
                pool.wait_ge(acc_zero, m + 1)
                if m >= 1:
                    l, j = divmod(m - 1, N_SUB)
                    pool.dma_start(ada_acc[0:1, 0, :], adab_v[l, 3 * j + 2:3 * j + 3, :]).then_inc(acc_bias, 16)
                if m < NSUBL:
                    l, j = divmod(m, N_SUB)
                    pool.dma_start(ada_acc[0:1, 1:3, :], adab_v[l:l + 1, 3 * j:3 * j + 2, :]).then_inc(acc_bias, 16)

            def inv_rms(q, wait, n, signal):
                pool.wait_ge(wait, n)
                link(nc.gpsimd.tensor_scalar(msq[:, q:q + 1], sumsq[:, q:q + 1], EPS, None, ALU.add))
                nc.gpsimd.tensor_tensor(rms[:, q:q + 1], msq[:, q:q + 1], neg_half[:], ALU.pow).then_inc(signal, 1)

            link(nc.gpsimd.memset(ident[:], 0.0))
            nc.gpsimd.memset(ones[:], 1.0).then_inc(consts, 1)
            nc.gpsimd.memset(neg_half[:], -0.5).then_inc(consts, 1)
            nc.gpsimd.affine_select(out=ident[:], in_=ident[:], compare_op=ALU.not_equal, fill=1.0, base=0,
                                    pattern=[[-1, P]], channel_multiplier=1).then_inc(consts, 1)
            acc_init(0)
            pool.wait_ge(consts, 3)
            for t in range(TOKS):
                inv_rms(2 + t, x_sq, t + 1, x_rms)
            pool.wait_ge(ws_copied, 2)
            nc.gpsimd.affine_select(out=ws_t[:], in_=ws_t[:], compare_op=ALU.is_ge, fill=0.0, base=0,
                                    pattern=[[0, GROUPS], [1, P]], channel_multiplier=-1).then_inc(ws_masked, 1)
            pool.dma_start(gate_w[:, 0], rg_w_a[0].rearrange("h d e -> d h e")).then_inc(gate_w_landed, 16)
            pool.dma_start(gate_w[:, 1], rg_w_x[0].rearrange("h d e -> d h e")).then_inc(gate_w_landed, 16)
            acc_init(1)

            for s in subs:
                i = s["i"]
                if i >= 1:
                    pool.wait_ge(x_new, 2 * i)
                pool.dma_start(gate_sc[:], norm_post[s["l"], s["j"]].partition_broadcast(P)).then_inc(post_landed, 16)
                if s["kind"] == "rg":
                    nc.gpsimd.memset(xb_pad[:, :, 0:CONV - 1], 0.0).then_inc(pads, 1)
                if s["kind"] == "gm":
                    pool.dma_start(gm_lg, gm_ln_g[0].partition_broadcast(P)).then_inc(ln_landed, 16)
                    pool.dma_start(gm_lb, gm_ln_b[0].partition_broadcast(P)).then_inc(ln_landed, 16)
                    for t in range(TOKS):
                        pool.wait_ge(ln_var, t + 1)
                        link(nc.gpsimd.tensor_scalar(ln_ve[:, t:t + 1], ln_mv[:, t, 1:2], EPS, None, ALU.add))
                        nc.gpsimd.tensor_tensor(ln_r[:, t:t + 1], ln_ve[:, t:t + 1], neg_half[:],
                                                ALU.pow).then_inc(ln_rstd, 1)
                if i + 2 <= NSUBL:
                    acc_init(i + 2)
                for t in range(TOKS):
                    inv_rms(t, y_sq, 2 * i + t + 1, y_rms)
                    if i + 1 < NSUBL:
                        inv_rms(2 + t, x_sq, 2 * (i + 1) + t + 1, x_rms)

        @block.scalar
        def _(act):
            def hi(u, n=0):
                s = u % SLOTS
                act.wait_ge(raw_landed[s], 16 * (u // SLOTS + 1) + n * (16 // SLOTS))
                if u >= SLOTS:
                    act.wait_ge(unit_used, u - SLOTS + 1 + n)
                nc.scalar.activation(w_hi[:, s, :], w_raw[:, s, :], ACT.Copy).then_inc(hi_done, 1)

            def round_ready(s, r, t, it=0, per=0):
                if t == 0:
                    act.wait_ge(in_ready, s["rb"] + r + 1 + it * per)
                else:
                    act.wait_ge(unit_used, s["ub"] + (r + 1) * ROUND + it * (per * ROUND))

            def silu(s, r, t, it=0, per=0):
                round_ready(s, r, t, it, per)
                p = r % 2
                nc.scalar.activation(stage[:, p, t, 0:HALF // 2], ps[:, 2 * p + t, 0:HALF // 2],
                                     ACT.Silu).then_inc(silu_done, 1)

            def pair_hi(s, n, it=0, per=0):
                act.wait_ge(pair_done, s["tb"] + n + 1 + it * per)
                b = 4 + n % 2
                src = ps[:, b, :].rearrange("p (k t) -> p k t", k=2)
                nc.scalar.activation(pair_of(z_hi, n, it, per), src, ACT.Copy).then_inc(zhi_done, 1)

            squares = []

            def mean_square(src, q, signal, n):
                if squares:
                    act.wait_ge(*squares[-1])
                squares.append((signal, n))
                nc.scalar.activation(junk, src, ACT.Square, scale=float(D) ** -0.5,
                                     accum_out=sumsq[:, q:q + 1]).then_inc(signal, 1)

            def y_square(s, t):
                if t == 0:
                    act.wait_ge(y_ready, s["i"] + 1)
                else:
                    act.wait_ge(unit_used, out_base(s) + s["kz"])
                b = y_bank(s, t)
                mean_square(ps[:, b:b + 2, :], t, y_sq, 2 * s["i"] + t + 1)

            def x_square(n, t):
                if n == 0:
                    act.wait_ge(x_landed, 16)
                else:
                    act.wait_ge(x_new, 2 * (n - 1) + t + 1)
                mean_square(xres[:, t, :].rearrange("p (a b) -> p a b", a=2), 2 + t, x_sq, 2 * n + t + 1)

            def h_hi_half(n, t, g):
                act.wait_ge(h_full, 2 * (2 * n + t) + g + 1)
                nc.scalar.activation(h_hi[:, 4 * g:4 * g + 4, t * P:(t + 1) * P], h_stage[:, 4 * g:4 * g + 4, :],
                                     ACT.Copy).then_inc(hhi_done, 1)

            for row, src in ((ROW_C, c.rearrange("b (k p) -> (b k) p", p=P)),
                             (ROW_CW, rg_conv_w.rearrange("l w (k p) -> (l w k) p", p=P)),
                             (ROW_CB, rg_conv_b.rearrange("l (k p) -> (l k) p", p=P)),
                             (ROW_BA, rg_b_a.rearrange("l (k p) -> (l k) p", p=P)),
                             (ROW_BX, rg_b_x.rearrange("l (k p) -> (l k) p", p=P)),
                             (ROW_LAM, rg_lambda.rearrange("l (k p) -> (l k) p", p=P)),
                             (ROW_BS, gm_b_s.rearrange("l g t -> (l g) t"))):
                act.dma_start(prm_rows[row:row + src.shape[0], :], src).then_inc(prm_landed, 16)
            act.dma_start(pre_g[:], norm_pre.rearrange("l j (p k) -> p (l j) k", p=P)).then_inc(pre_landed, 16)
            act.dma_start(xres[:], x[0].rearrange("(t p) d -> p t d", p=P)).then_inc(x_landed, 16)
            act.dma_start(gate_w[:, 0], gm_w_s[0].rearrange("g t s -> t g s")).then_inc(ws_landed, 16)

            act.wait_ge(prm_done, 1)
            nc.scalar.activation(c_act[:, :, 0], prm[:, ROW_C:ROW_C + KD], ACT.Silu).then_inc(c_done, 1)
            for t in range(TOKS):
                x_square(0, t)
            act.wait_ge(lam_abs, 1)
            nc.scalar.activation(sp[:, LAM_E, :], sp[:, LAM_T, :], ACT.Exp, scale=-1.0).then_inc(lam_exp, 1)
            for u in range(SLOTS):
                hi(u)
            for t in range(TOKS):
                for g in range(2):
                    h_hi_half(0, t, g)

            for s in subs:
                i, kind, ub, ob, R = s["i"], s["kind"], s["ub"], out_base(s), s["rounds"]
                for q in range(4):
                    hi(ub + 4 + q)
                if kind == "ffn":
                    with act.Fori(0, (R - 1) // 2) as it:
                        for r in (1, 2):
                            for t in range(TOKS):
                                silu(s, r - 1, t, it, 2)
                            for q in range(4):
                                if q == 3:
                                    pair_hi(s, r - 1, it, 2)
                                hi(ub + 4 * r + 4 + q, n=it * 8)
                    for t in range(TOKS):
                        silu(s, R - 1, t)
                    hi(ob + 4)
                    hi(ob + 5)
                    pair_hi(s, R - 1)
                    done = 6
                elif kind == "rg":
                    def stage_round(r, f):
                        for t in range(TOKS):
                            round_ready(s, r, t)
                            nc.scalar.activation(stage[:, r % 2, t, :], ps[:, 2 * (r % 2) + t, :],
                                                 f).then_inc(mix_staged, 1)

                    def take_pair(n):
                        act.wait_ge(pair_done, s["tb"] + n + 1)
                        src = ps[:, 4 + n % 2, :].rearrange("p (k t) -> p k t", k=2)
                        if n == 0:
                            act.wait_ge(pads, 1)
                        dst = (xb_pad[:, 2 * n:2 * n + 2, CONV - 1:] if n < KD // 2 else
                               rg_g[:, 2 * n - KD:2 * n - KD + 2, :])
                        nc.scalar.activation(dst, src, ACT.Copy).then_inc(rg_pair_read, 1)

                    def gate_tanh(h):
                        act.wait_ge(gates_done, h + 1)
                        b = 6 + h % 2
                        if h >= 4:
                            act.wait_ge(m2_done, h - 3)
                        nc.scalar.activation(rg_a[:, h, :], ps[:, b, 0:SEQ], ACT.Tanh, scale=0.5,
                                             bias=sp[:, HBA, h:h + 1]).then_inc(act_step, 1)
                        nc.scalar.activation(gate_t[:, h % 4, :], ps[:, b, SEQ:2 * SEQ], ACT.Tanh, scale=0.5,
                                             bias=sp[:, HBX, h:h + 1]).then_inc(gates_read, 1)

                    def decay(h):
                        act.wait_ge(act_step, h + 1)
                        nc.scalar.activation(rg_m[:, h, :], rg_a[:, h, :], ACT.Tanh, scale=sp[:, SP_P, h:h + 1],
                                             bias=sp[:, SP_P, h:h + 1]).then_inc(tan_done, 1)
                        act.wait_ge(tan_done, h + 1)
                        nc.scalar.activation(rg_a[:, h, :], rg_a[:, h, :], ACT.Exp, scale=sp[:, SP_N, h:h + 1],
                                             bias=sp[:, SP_N, h:h + 1]).then_inc(exp_done, 1)

                    for r in range(1, R):
                        stage_round(r - 1, ACT.Copy if r - 1 < 2 else ACT.Gelu_apprx_tanh)
                        for q in range(4):
                            if q == 3:
                                take_pair(2 * r - 2)
                                take_pair(2 * r - 1)
                            hi(ub + 4 * r + 4 + q)
                    stage_round(R - 1, ACT.Gelu_apprx_tanh)
                    for h in range(4):
                        gate_tanh(h)
                        decay(h)
                    take_pair(2 * R - 2)
                    take_pair(2 * R - 1)
                    for h in range(4, HEADS):
                        gate_tanh(h)
                        decay(h)
                    for g in range(2):
                        act.wait_ge(m2_done, 4 * g + 4)
                        nc.scalar.activation(rg_m[:, 4 * g:4 * g + 4, :], rg_m[:, 4 * g:4 * g + 4, :], ACT.Sqrt,
                                             scale=0.25).then_inc(mult_done, 1)
                    for n in range(KD // 2):
                        act.wait_ge(hs_done, n + 1)
                        nc.scalar.activation(z_hi[:, 2 * n:2 * n + 2, :], rg_x[:, 2 * n:2 * n + 2, :],
                                             ACT.Copy).then_inc(zhi_done, 1)
                    done = 4
                else:
                    def gelu_v(r):
                        for t in range(TOKS):
                            round_ready(s, r, t)
                            nc.scalar.activation(gm_v[:, t, r * HALF:(r + 1) * HALF], ps[:, 2 * (r % 2) + t, :],
                                                 ACT.Gelu_apprx_tanh).then_inc(mix_staged, 1)

                    def gelu_u(r):
                        for t in range(TOKS):
                            round_ready(s, r, t)
                            nc.scalar.activation(stage[:, r % 2, t, :], ps[:, 2 * (r % 2) + t, :],
                                                 ACT.Gelu_apprx_tanh).then_inc(mix_staged, 1)

                    def hi4(r, pairs_at=None):
                        for q in range(4):
                            if q == 3 and pairs_at is not None:
                                pair_hi(s, pairs_at)
                                pair_hi(s, pairs_at + 1)
                            hi(ub + 4 * r + 4 + q)

                    for r in range(1, 5):
                        gelu_v(r - 1)
                        hi4(r)
                    gelu_u(4)
                    hi4(5)
                    for n in range(TOKS * GROUPS // 2):
                        t, g2 = divmod(n, GROUPS // 2)
                        act.wait_ge(sp_done, n + 1)
                        for g in (2 * g2, 2 * g2 + 1):
                            last = nc.scalar.activation(gm_v[:, t, g * GD:(g + 1) * GD],
                                                        ps[:, 6 + n % 2, (g % 2) * GD:(g % 2) * GD + GD],
                                                        ACT.Identity, bias=prm[:, ROW_BS + g:ROW_BS + g + 1])
                        last.then_inc(sp_read, 1)
                    gelu_u(5)
                    hi4(6, 0)
                    gelu_u(6)
                    hi4(7, 2)
                    gelu_u(7)
                    hi(ob + 4)
                    hi(ob + 5)
                    pair_hi(s, 4)
                    pair_hi(s, 5)
                    hi(ob + 6)
                    hi(ob + 7)
                    pair_hi(s, 6)
                    pair_hi(s, 7)
                    done = 8

                left = s["kz"] - done
                if left >= 8:
                    with act.Fori(0, left // 4) as it:
                        for q in range(4):
                            hi(ob + done + q, n=it * 4)
                    done += left // 4 * 4
                for o in range(done, s["kz"]):
                    hi(ob + o)
                nxt = ob + s["kz"]
                if i + 1 < NSUBL:
                    y_square(s, 0)
                    hi(nxt)
                    x_square(i + 1, 0)
                    hi(nxt + 1)
                    y_square(s, 1)
                    for g in range(2):
                        h_hi_half(i + 1, 0, g)
                    hi(nxt + 2)
                    hi(nxt + 3)
                    x_square(i + 1, 1)
                    for g in range(2):
                        h_hi_half(i + 1, 1, g)
                else:
                    for t in range(TOKS):
                        y_square(s, t)

        @block.vector
        def _(dve):
            steps = [0]

            def link(ins):
                steps[0] += 1
                ins.then_inc(dve_step, 1)
                dve.wait_ge(dve_step, steps[0])

            def lo(u, n=0):
                s = u % SLOTS
                dve.wait_ge(hi_done, u + 1 + n)
                nc.vector.tensor_tensor(w_lo[:, s, :], w_raw[:, s, :], w_hi[:, s, :].bitcast(F32),
                                        ALU.subtract).then_inc(lo_done, 1)

            def ada(i, k, it=0):
                n = 3 if i + 1 < NSUBL else 1
                before = 3 * i * KD
                if k == 0:
                    dve.wait_ge(acc_bias, 16 * (1 + 2 * i + (2 if i + 1 < NSUBL else 1)))
                for q in range(n):
                    dve.wait_ge(ada_landed[q], 16 * (i * KD + k + 1) + it * 16)
                    if k >= 1:
                        dve.wait_ge(ada_added, before + n * (k - 1) + q + 1 + it * n)
                    nc.vector.scalar_tensor_tensor(out=ada_acc[:, q, :], in0=ada_raw[:, q, :],
                                                   scalar=c_act[:, it + k, :], in1=ada_acc[:, q, :],
                                                   op0=ALU.mult, op1=ALU.add).then_inc(ada_added, 1)

            def gate_up(s, r, t, it=0, per=0):
                dve.wait_ge(silu_done, 2 * (s["sb"] + r) + t + 1 + it * (2 * per))
                p = r % 2
                nc.vector.tensor_tensor(stage[:, p, t, HALF // 2:], ps[:, 2 * p + t, HALF // 2:],
                                        stage[:, p, t, 0:HALF // 2], ALU.mult).then_inc(z_staged, 1)

            def pair_lo(s, n, it=0, per=0):
                dve.wait_ge(zhi_done, s["zb"] + n + 1 + it * per)
                src = ps[:, 4 + n % 2, :].rearrange("p (k t) -> p k t", k=2)
                nc.vector.tensor_tensor(pair_of(z_lo, n, it, per), src, pair_of(z_hi, n, it, per).bitcast(F32),
                                        ALU.subtract).then_inc(z_ready, 1)

            def post(s, t):
                dve.wait_ge(y_rms, 2 * s["i"] + t + 1)
                if t == 1:
                    if s["i"] + 1 < NSUBL:
                        dve.wait_ge(h_ready, 4 * (s["i"] + 1) + 2)
                    else:
                        dve.wait_ge(x_new, 2 * s["i"] + 1)
                b = y_bank(s, t)
                nc.vector.scalar_tensor_tensor(out=tmp2, in0=ps[:, b:b + 2, :], scalar=rms[:, t:t + 1],
                                               in1=gate_sc[:].rearrange("p (a b) -> p a b", a=2),
                                               op0=ALU.mult, op1=ALU.mult).then_inc(y_scaled, 1)
                dve.wait_ge(y_scaled, 2 * s["i"] + t + 1)
                nc.vector.tensor_tensor(xres[:, t, :].rearrange("p (a b) -> p a b", a=2),
                                        xres[:, t, :].rearrange("p (a b) -> p a b", a=2), tmp2,
                                        ALU.add).then_inc(x_new, 1)

            def normed(n, t):
                if n == 0:
                    dve.wait_ge(x_landed, 16)
                dve.wait_ge(x_rms, 2 * n + t + 1)
                nc.vector.tensor_scalar(xn_stage, xres[:, t, :], rms[:, 2 + t:3 + t], None,
                                        ALU.mult).then_inc(x_normed, 1)

            def modulated(n, t, g):
                dve.wait_ge(x_turned, 2 * (2 * n + t) + g + 1)
                for k in range(4 * g, 4 * g + 4):
                    last = nc.vector.tensor_scalar(h_stage[:, k, :], ps[:, 4 + g, (k % 4) * P:(k % 4 + 1) * P],
                                                   mod_a[:, k:k + 1], mod_b[:, k:k + 1], ALU.mult, ALU.add)
                last.then_inc(h_full, 1)

            def h_lo_half(n, t, g):
                dve.wait_ge(hhi_done, 2 * (2 * n + t) + g + 1)
                sl = (slice(None), slice(4 * g, 4 * g + 4), slice(t * P, (t + 1) * P))
                nc.vector.tensor_tensor(h_lo[sl], h_stage[:, 4 * g:4 * g + 4, :], h_hi[sl].bitcast(F32),
                                        ALU.subtract).then_inc(h_ready, 1)

            def take_mod(m, s):
                dve.wait_ge(mod_summed, m + 1)
                if m >= 1:
                    b = mod_bank(s)
                    dve.wait_ge(post_landed, 16 * m)
                    last = nc.vector.scalar_tensor_tensor(out=gate_sc[:].rearrange("p (a b) -> p a b", a=2),
                                                          in0=ps[:, b:b + 2, :], scalar=float(s["res"]),
                                                          in1=gate_sc[:].rearrange("p (a b) -> p a b", a=2),
                                                          op0=ALU.mult, op1=ALU.mult)
                if m == 0:
                    dve.wait_ge(pre_landed, 16)
                if m < NSUBL:
                    nc.vector.tensor_copy(mod_b[:], ps[:, 4, 0:KD])
                    last = nc.vector.scalar_tensor_tensor(out=mod_a[:], in0=ps[:, 4, KD:2 * KD], scalar=1.0,
                                                          in1=pre_g[:, m, :],
                                                          op0=ALU.add, op1=ALU.mult)
                last.then_inc(mod_set, 1)
                dve.wait_ge(mod_set, m + 1)

            dve.wait_ge(prm_turned, 1)
            nc.vector.tensor_copy(prm[:], ps[:, 0, 0:ROWS]).then_inc(prm_done, 1)
            dve.wait_ge(prm_done, 1)
            lam = prm[:, ROW_LAM:ROW_LAM + KD]
            link(nc.vector.tensor_scalar(sp[:, LAM_W, :], lam, -1.0, None, ALU.mult))
            nc.vector.tensor_tensor(sp[:, LAM_T, :], lam, sp[:, LAM_W, :], ALU.max).then_inc(lam_abs, 1)
            nc.vector.tensor_scalar(sp[:, HBA, :], prm[:, ROW_BA:ROW_BA + KD], 0.5, None, ALU.mult)
            nc.vector.tensor_scalar(sp[:, HBX, :], prm[:, ROW_BX:ROW_BX + KD], 0.5, None, ALU.mult)
            dve.wait_ge(c_done, 1)
            dve.wait_ge(acc_bias, 16)
            for k in range(KD):
                dve.wait_ge(land_full[k % LAND], 32 * (k // LAND + 1))
                for q in range(2):
                    if k >= 1:
                        dve.wait_ge(land_added, 2 * k - 2 + q + 1)
                    nc.vector.scalar_tensor_tensor(out=ada_acc[:, 1 + q, :], in0=land[:, k % LAND, q, :],
                                                   scalar=c_act[:, k, :], in1=ada_acc[:, 1 + q, :],
                                                   op0=ALU.mult, op1=ALU.add).then_inc(land_added, 1)
                if k == 1:
                    for g in range(2):
                        dve.wait_ge(ws_turned, g + 1)
                        nc.vector.tensor_copy(ws_t[:, 4 * g:4 * g + 4, :],
                                              ps[:, 1 + g, :].rearrange("p (g t) -> p g t", g=4)).then_inc(ws_copied, 1)
                if k == 2:
                    dve.wait_ge(lam_exp, 1)
                    e, w, w2, q_, t_ = (sp[:, z, :] for z in (LAM_E, LAM_W, LAM_W2, LAM_Q, LAM_T))
                    link(nc.vector.tensor_scalar(w2, e, 2.0, None, ALU.add))
                    link(nc.vector.reciprocal(q_, w2))
                    link(nc.vector.tensor_tensor(w, e, q_, ALU.mult))
                    link(nc.vector.tensor_tensor(w2, w, w, ALU.mult))
                    link(nc.vector.tensor_scalar(q_, w2, 1.0 / 15, None, ALU.mult))
                    for d in (13, 11, 9, 7, 5, 3):
                        link(nc.vector.scalar_tensor_tensor(out=q_, in0=q_, scalar=1.0 / d, in1=w2,
                                                            op0=ALU.add, op1=ALU.mult))
                    link(nc.vector.scalar_tensor_tensor(out=w, in0=q_, scalar=1.0, in1=w, op0=ALU.add, op1=ALU.mult))
                    link(nc.vector.tensor_scalar(t_, lam, -1.0, 0.0, ALU.mult, ALU.max))
                    link(nc.vector.scalar_tensor_tensor(out=q_, in0=w, scalar=2.0, in1=t_, op0=ALU.mult, op1=ALU.add))
                    nc.vector.tensor_scalar(sp[:, SP_P, :], q_, 4.0, None, ALU.mult)
                    link(nc.vector.tensor_scalar(sp[:, SP_N, :], q_, -4.0, None, ALU.mult))
            for u in range(SLOTS):
                lo(u)
            normed(0, 0)
            take_mod(0, None)
            for t in range(TOKS):
                for g in range(2):
                    modulated(0, t, g)
                for g in range(2):
                    h_lo_half(0, t, g)
                if t == 0:
                    normed(0, 1)

            for s in subs:
                i, kind, ub, ob, R = s["i"], s["kind"], s["ub"], out_base(s), s["rounds"]
                for q in range(4):
                    lo(ub + 4 + q)
                ada(i, 0)
                if kind == "ffn":
                    with dve.Fori(0, (R - 1) // 2) as it:
                        for r in (1, 2):
                            for t in range(TOKS):
                                gate_up(s, r - 1, t, it, 2)
                            for q in range(4):
                                if q == 3:
                                    pair_lo(s, r - 1, it, 2)
                                lo(ub + 4 * r + 4 + q, n=it * 8)
                            if r == 1:
                                ada(i, 1, it)
                    for t in range(TOKS):
                        gate_up(s, R - 1, t)
                    ada(i, 6)
                    lo(ob + 4)
                    lo(ob + 5)
                    pair_lo(s, R - 1)
                    done = 6
                elif kind == "rg":
                    def conv(heads):
                        dve.wait_ge(rg_pair_read, heads[-1] // 2 + 1)
                        for k in range(CONV):
                            for h in heads:
                                w = prm[:, ROW_CW + k * KD + h:ROW_CW + k * KD + h + 1]
                                if k == 0:
                                    ins = nc.vector.tensor_scalar(rg_x[:, h, :], xb_pad[:, h, 0:SEQ], w,
                                                                  prm[:, ROW_CB + h:ROW_CB + h + 1],
                                                                  ALU.mult, ALU.add)
                                else:
                                    dve.wait_ge(conv_done, conv_n[0] - len(heads) + 1)
                                    ins = nc.vector.scalar_tensor_tensor(
                                        out=rg_x[:, h, :], in0=xb_pad[:, h, k:k + SEQ], scalar=w,
                                        in1=rg_x[:, h, :], op0=ALU.mult, op1=ALU.add)
                                ins.then_inc(conv_done, 1)
                                conv_n[0] += 1

                    conv_n = [0]

                    def gate_math(h):
                        dve.wait_ge(gates_read, h + 1)
                        link(nc.vector.scalar_tensor_tensor(out=rg_x[:, h, :], in0=gate_t[:, h % 4, :], scalar=1.0,
                                                            in1=rg_x[:, h, :], op0=ALU.add, op1=ALU.mult))
                        dve.wait_ge(exp_done, h + 1)
                        link(nc.vector.tensor_tensor(gate_t[:, h % 4, :], rg_a[:, h, :], rg_a[:, h, :], ALU.mult))
                        nc.vector.scalar_tensor_tensor(out=rg_m[:, h, :], in0=gate_t[:, h % 4, :], scalar=1.0,
                                                       in1=rg_m[:, h, :], op0=ALU.add,
                                                       op1=ALU.mult).then_inc(m2_done, 1)

                    for r in range(1, R):
                        for q in range(4):
                            lo(ub + 4 * r + 4 + q)
                            if q % 2 == 1:
                                ada(i, 2 * r - 1 + q // 2)
                        if r <= 2:
                            conv(range(4 * r - 4, 4 * r))
                    for h in range(HEADS):
                        gate_math(h)
                    for g in range(2):
                        dve.wait_ge(mult_done, g + 1)
                        hs4 = (slice(None), slice(4 * g, 4 * g + 4), slice(None))
                        link(nc.vector.tensor_tensor(rg_x[hs4], rg_m[hs4], rg_x[hs4], ALU.mult))
                        for h in range(4 * g, 4 * g + 4):
                            ins = nc.vector.tensor_tensor_scan(rg_m[:, h, :], rg_a[:, h, :], rg_x[:, h, :], 0.0,
                                                               ALU.mult, ALU.add)
                            if h % 4 == 3:
                                link(ins)
                        for n in (2 * g, 2 * g + 1):
                            pr = (slice(None), slice(2 * n, 2 * n + 2), slice(None))
                            if n == 0:
                                dve.wait_ge(rg_pair_read, 2 * R)
                            nc.vector.tensor_tensor(rg_x[pr], rg_m[pr], rg_g[pr], ALU.mult).then_inc(hs_done, 1)
                        for n in (2 * g, 2 * g + 1):
                            pr = (slice(None), slice(2 * n, 2 * n + 2), slice(None))
                            dve.wait_ge(zhi_done, s["zb"] + n + 1)
                            nc.vector.tensor_tensor(z_lo[pr], rg_x[pr], z_hi[pr].bitcast(F32),
                                                    ALU.subtract).then_inc(z_ready, 1)
                    done = 4
                else:
                    def v_stats(r):
                        for t in range(TOKS):
                            dve.wait_ge(mix_staged, s["mb"] + 2 * r + t + 1)
                            nc.vector.bn_stats(bn[:, t, r, :], gm_v[:, t, r * HALF:(r + 1) * HALF]).then_inc(v_normed, 1)

                    def u_gate(r):
                        if r == 4:
                            dve.wait_ge(sp_read, TOKS * GROUPS // 2)
                        for t in range(TOKS):
                            dve.wait_ge(mix_staged, s["mb"] + 2 * r + t + 1)
                            nc.vector.tensor_tensor(stage[:, r % 2, t, :], stage[:, r % 2, t, :],
                                                    gm_v[:, t, (r - 4) * HALF:(r - 3) * HALF],
                                                    ALU.mult).then_inc(u_staged, 1)

                    def lo4(r, pairs_at=None):
                        for q in range(4):
                            if q == 3 and pairs_at is not None:
                                pair_lo(s, pairs_at)
                                pair_lo(s, pairs_at + 1)
                            lo(ub + 4 * r + 4 + q)

                    def layer_norm(t):
                        link(nc.vector.scalar_tensor_tensor(out=gm_v[:, t, :], in0=gm_v[:, t, :],
                                                            scalar=ln_mv[:, t, 0:1], in1=gm_lg,
                                                            op0=ALU.subtract, op1=ALU.mult))
                        dve.wait_ge(ln_rstd, t + 1)
                        nc.vector.scalar_tensor_tensor(out=gm_v[:, t, :], in0=gm_v[:, t, :], scalar=ln_r[:, t:t + 1],
                                                       in1=gm_lb, op0=ALU.mult, op1=ALU.add).then_inc(v_normed, 1)

                    for r in range(1, 4):
                        v_stats(r - 1)
                        lo4(r)
                        ada(i, r)
                    v_stats(3)
                    dve.wait_ge(v_normed, 4 * TOKS)
                    for t in range(TOKS):
                        nc.vector.bn_aggr(ln_mv[:, t, :], bn[:, t, :, :]).then_inc(ln_var, 1)
                    dve.wait_ge(ln_var, 2)
                    dve.wait_ge(ln_landed, 32)
                    lo(ub + 20)
                    layer_norm(0)
                    lo(ub + 21)
                    lo(ub + 22)
                    layer_norm(1)
                    lo(ub + 23)
                    lo4(5)
                    ada(i, 4)
                    u_gate(4)
                    u_gate(5)
                    lo4(6, 0)
                    ada(i, 5)
                    u_gate(6)
                    lo4(7, 2)
                    u_gate(7)
                    ada(i, 6)
                    lo(ob + 4)
                    lo(ob + 5)
                    pair_lo(s, 4)
                    pair_lo(s, 5)
                    lo(ob + 6)
                    lo(ob + 7)
                    pair_lo(s, 6)
                    pair_lo(s, 7)
                    done = 8

                if s["kz"] - done > 4:
                    for q in range(4):
                        lo(ob + done + q)
                    done += 4
                ada(i, 7)
                left = s["kz"] - done
                if left >= 8:
                    with dve.Fori(0, left // 4) as it:
                        for q in range(4):
                            lo(ob + done + q, n=it * 4)
                    done += left // 4 * 4
                for o in range(done, s["kz"]):
                    lo(ob + o)
                take_mod(i + 1, s)

                nxt = ob + s["kz"]
                post(s, 0)
                if i + 1 < NSUBL:
                    lo(nxt)
                    normed(i + 1, 0)
                    lo(nxt + 1)
                    for g in range(2):
                        modulated(i + 1, 0, g)
                    for g in range(2):
                        h_lo_half(i + 1, 0, g)
                    lo(nxt + 2)
                    lo(nxt + 3)
                    post(s, 1)
                    normed(i + 1, 1)
                    for g in range(2):
                        modulated(i + 1, 1, g)
                    for g in range(2):
                        h_lo_half(i + 1, 1, g)
                else:
                    post(s, 1)

        @block.tensor
        def _(pe):
            def three(dst, hi_, lo_, whi, wlo, start, stop):
                nc.tensor.matmul(dst, hi_, whi, start=start, stop=False)
                nc.tensor.matmul(dst, hi_, wlo, start=False, stop=False)
                return nc.tensor.matmul(dst, lo_, whi, start=False, stop=stop)

            def in_unit(u, q, p, toks, n=0):
                if 0 in toks:
                    pe.wait_ge(lo_done, u + 1 + n)
                w = u % SLOTS
                for k in (2 * q, 2 * q + 1):
                    cols = slice((k % 2) * HALF, (k % 2 + 1) * HALF)
                    for t in toks:
                        tok = slice(t * P, (t + 1) * P)
                        last = three(ps[:, 2 * p + t, :], h_hi[:, k, tok], h_lo[:, k, tok],
                                     w_hi[:, w, cols], w_lo[:, w, cols], k == 0, k == KD - 1)
                        if t == 0 and k == KD - 1:
                            last.then_inc(in_ready, 1)
                if 1 in toks:
                    last.then_inc(unit_used, 1)

            def first_round(s):
                for t in range(TOKS):
                    for q in range(ROUND):
                        if s["i"] > 0 and t == 0 and q == TURN_AT:
                            turn_x(s["i"], 1)
                        if q % 2 == 0:
                            pe.wait_ge(h_ready, 2 * (2 * s["i"] + t) + q // 2 + 1)
                        in_unit(s["ub"] + q, q, 0, (t,))

            def turn(n, p, col0):
                for t in range(TOKS):
                    for m in range(2):
                        last = nc.tensor.transpose(ps[:, 4 + n % 2, m * SEQ + t * P:m * SEQ + (t + 1) * P],
                                                   stage[:, p, t, col0 + m * P:col0 + (m + 1) * P], ident[:])
                last.then_inc(pair_done, 1)

            def turn_ffn(s, r, it=0, per=0):
                pe.wait_ge(z_staged, 2 * (s["sb"] + r) + 2 + it * (2 * per))
                turn(r, r % 2, HALF // 2)

            def out_unit(s, o, toks):
                u = out_base(s) + o
                if 0 in toks:
                    pe.wait_ge(lo_done, u + 1)
                    if o % 2 == 0:
                        pe.wait_ge(z_ready, s["zb"] + o // 2 + 1)
                w = u % SLOTS
                for t in toks:
                    tok = slice(t * P, (t + 1) * P)
                    for g in range(2):
                        cols = slice(g * HALF, (g + 1) * HALF)
                        last = three(ps[:, y_bank(s, t) + g, :], z_hi[:, o, tok], z_lo[:, o, tok],
                                     w_hi[:, w, cols], w_lo[:, w, cols], o == 0, o == s["kz"] - 1)
                    if t == 0 and o == s["kz"] - 1:
                        last.then_inc(y_ready, 1)
                if 1 in toks:
                    last.then_inc(unit_used, 1)

            def sum_mod(m, b):
                if m == 0:
                    pe.wait_ge(land_added, 2 * KD)
                else:
                    pe.wait_ge(ada_added, 3 * KD * m if m < NSUBL else 3 * KD * (m - 1) + KD)
                if m >= 1:
                    for g in range(2):
                        last = nc.tensor.matmul(ps[:, b + g, :], ones[:], ada_acc[:, 0, g * HALF:(g + 1) * HALF],
                                                start=True, stop=True)
                if m < NSUBL:
                    for q in range(2):
                        for k in range(KD):
                            last = nc.tensor.matmul(ps[:, 4, q * KD + k:q * KD + k + 1],
                                                    ada_acc[:, 1 + q, k:D:KD], ones[:, 0:1],
                                                    start=True, stop=True)
                last.then_inc(mod_summed, 1)

            def turn_x(n, t):
                pe.wait_ge(x_normed, 2 * n + t + 1)
                if n >= 0 and 2 * n + t >= 1:
                    pe.wait_ge(h_full, 2 * (2 * n + t))
                if t == 0:
                    pe.wait_ge(mod_set, n + 1)
                for g in range(2):
                    for k in range(4):
                        last = nc.tensor.transpose(ps[:, 4 + g, k * P:(k + 1) * P],
                                                   xn_stage[:, 4 * g + k:D:KD], ident[:])
                    last.then_inc(x_turned, 1)

            pe.wait_ge(consts, 3)
            pe.wait_ge(prm_landed, 16 * 7)
            nc.tensor.transpose(ps[:, 0, 0:ROWS], prm_rows[:], ident[0:ROWS, 0:ROWS]).then_inc(prm_turned, 1)
            pe.wait_ge(ws_landed, 16)
            for g in range(GROUPS):
                last = nc.tensor.transpose(ps[:, 1 + g // 4, (g % 4) * P:(g % 4 + 1) * P], gate_w[:, 0, g, :], ident[:])
                if g % 4 == 3:
                    last.then_inc(ws_turned, 1)
            sum_mod(0, 0)
            turn_x(0, 0)
            turn_x(0, 1)

            for s in subs:
                i, kind, ub, R = s["i"], s["kind"], s["ub"], s["rounds"]
                first_round(s)
                extra = {}
                if kind == "ffn":
                    with pe.Fori(0, (R - 1) // 2) as it:
                        for r in (1, 2):
                            for q in range(ROUND):
                                if q == 3:
                                    turn_ffn(s, r - 1, it, 2)
                                in_unit(ub + 4 * r + q, q, r % 2, (0, 1), n=it * 8)
                    extra[1] = lambda: turn_ffn(s, R - 1)
                elif kind == "rg":
                    def rg_turn(r):
                        pe.wait_ge(mix_staged, s["mb"] + 2 * r + 2)
                        for m in range(2):
                            n = 2 * r + m
                            if n >= 2:
                                pe.wait_ge(rg_pair_read, n - 1)
                            turn(n, r % 2, m * 2 * P)

                    def gates(h):
                        if h == 0:
                            pe.wait_ge(gate_w_landed, 32)
                        pe.wait_ge(conv_done, 16 * (h // 4) + 12 + h % 4 + 1)
                        if h >= 2:
                            pe.wait_ge(gates_read, h - 1)
                        for g in range(2):
                            last = nc.tensor.matmul(ps[:, 6 + h % 2, g * SEQ:(g + 1) * SEQ], gate_w[:, g, h, :],
                                                    rg_x[:, h, :], start=True, stop=True)
                        last.then_inc(gates_done, 1)

                    for r in range(1, R):
                        if r >= 2:
                            pe.wait_ge(mix_staged, s["mb"] + 2 * (r - 2) + 2)
                        for q in range(ROUND):
                            if q == 3:
                                rg_turn(r - 1)
                            in_unit(ub + 4 * r + q, q, r % 2, (0, 1))
                    for h in range(2):
                        gates(h)
                    rg_turn(R - 1)
                    for h in range(2, HEADS):
                        gates(h)
                else:
                    def gm_turn(r):
                        pe.wait_ge(u_staged, 2 * (r - 4) + 2)
                        for m in range(2):
                            n = 2 * (r - 4) + m
                            if n >= 2:
                                pe.wait_ge(z_ready, s["zb"] + n - 1)
                            turn(n, r % 2, m * 2 * P)

                    def spatial():
                        pe.wait_ge(ws_masked, 1)
                        for n in range(TOKS * GROUPS // 2):
                            t, g2 = divmod(n, GROUPS // 2)
                            if g2 == 0:
                                pe.wait_ge(v_normed, 4 * TOKS + t + 1)
                            if n >= 2:
                                pe.wait_ge(sp_read, n - 1)
                            for g in (2 * g2, 2 * g2 + 1):
                                last = nc.tensor.matmul(ps[:, 6 + n % 2, (g % 2) * GD:(g % 2) * GD + GD], ws_t[:, g, :],
                                                        gm_v[:, t, g * GD:(g + 1) * GD], start=True, stop=True)
                            last.then_inc(sp_done, 1)

                    for r in range(1, R):
                        if r >= 2:
                            pe.wait_ge(mix_staged, s["mb"] + 2 * (r - 2) + 2)
                        if r == 6:
                            spatial()
                        for q in range(ROUND):
                            if q == 3 and r >= 6:
                                gm_turn(r - 2)
                            in_unit(ub + 4 * r + q, q, r % 2, (0, 1))
                    extra[1] = lambda: gm_turn(R - 2)
                    extra[3] = lambda: gm_turn(R - 1)

                if kind == "ffn":
                    pe.wait_ge(z_staged, 2 * (s["sb"] + R - 2) + 2)
                else:
                    pe.wait_ge(mix_staged, s["mb"] + 2 * (R - 2) + 2)
                kz = s["kz"]
                mod_at = MOD_AT[kind]
                for o in range(kz - TAIL):
                    out_unit(s, o, (0, 1))
                    if o in extra:
                        extra[o]()
                    if o == mod_at:
                        sum_mod(i + 1, mod_bank(s))
                for t in range(TOKS):
                    for o in range(kz - TAIL, kz):
                        out_unit(s, o, (t,))
                        if t == 0 and o == mod_at:
                            sum_mod(i + 1, mod_bank(s))
                if i + 1 < NSUBL:
                    turn_x(i + 1, 0)


_INS = ["x", "c", "ada_w", "ada_b", "norm_pre", "norm_post", "ffn_w_in", "ffn_w_out",
        "rg_w_in", "rg_conv_w", "rg_conv_b", "rg_w_a", "rg_b_a", "rg_w_x", "rg_b_x",
        "rg_lambda", "rg_w_out", "gm_w_in", "gm_ln_g", "gm_ln_b", "gm_w_s", "gm_b_s",
        "gm_w_out"]


def kernel(**inputs):
    import numpy as _np
    import concourse.bacc as _bacc
    from concourse import mybir as _mybir
    from concourse.bass_utils import run_bass_kernel_spmd as _run

    nc = _bacc.Bacc("TRN2", target_bir_lowering=False, num_devices=1)
    arrays, args = {}, []
    for name in _INS:
        a = _np.ascontiguousarray(inputs[name])
        arrays[f"in_{name}_dram"] = a
        args.append(nc.dram_tensor(f"in_{name}_dram", a.shape, _mybir.dt.from_np(a.dtype),
                                   kind="ExternalInput").ap())
    shape = arrays["in_x_dram"].shape
    args.append(nc.dram_tensor("out_0_dram", shape, _mybir.dt.float32, kind="ExternalOutput").ap())
    trunk(nc, *args)
    r = _run(nc, [arrays], core_ids=[0])
    return r.results[0]["out_0_dram"]
```

```python
from contextlib import ExitStack

import concourse.bass as bass
from concourse import mybir

ALU = mybir.AluOpType
ACT = mybir.ActivationFunctionType
F32 = mybir.dt.float32
F32R = mybir.dt.float32r

P = 128
EPS = 1e-6


def trunk(nc, x, c, ada_w, ada_b, norm_pre, norm_post, ffn_w_in, ffn_w_out,
          rg_w_in, rg_conv_w, rg_conv_b, rg_w_a, rg_b_a, rg_w_x, rg_b_x,
          rg_lambda, rg_w_out, gm_w_in, gm_ln_g, gm_ln_b, gm_w_s, gm_b_s,
          gm_w_out, out):
    _, SEQ, D = x.shape
    TOKS = SEQ // P
    KD = D // P
    D_FF = ffn_w_out.shape[2]
    KF = D_FF // P
    HEADS, CONV = rg_w_a.shape[1], rg_conv_w.shape[1]
    D_G = gm_w_out.shape[1]
    GROUPS = gm_w_s.shape[1]
    GD = D_G // GROUPS
    DEPTH = ada_w.shape[0]
    N_SUB = 3
    NSUBL = DEPTH * N_SUB
    assert (TOKS, KD, KF % 2, CONV, HEADS, GROUPS, NSUBL) == (2, 8, 0, 4, KD, 8, 6)

    UNIT = 1024
    HALF = 512
    SLOTS = 8
    ROUND = 4
    HEAD = 2
    APART = 6
    TAIL = SLOTS
    TURN_AT = 4
    assert HEAD * ROUND == SLOTS

    subs = []
    units = in_rounds = silus = mixed = pairs = zpairs = 0
    for i in range(NSUBL):
        l, j = divmod(i, N_SUB)
        kind = "ffn" if j != 1 else ("rg" if l % 2 == 0 else "gm")
        kz = {"ffn": KF, "rg": KD, "gm": D_G // P}[kind]
        rounds = {"ffn": D_FF // (HALF // 2), "rg": 2 * D // HALF, "gm": 2 * D_G // HALF}[kind]
        n_pairs = {"ffn": KF // 2, "rg": KD, "gm": kz // 2}[kind]
        subs.append(dict(i=i, l=l, j=j, kind=kind, kz=kz, rounds=rounds, res=1.0 if j == 1 else 0.5,
                         ub=units, rb=in_rounds, sb=silus, mb=mixed, tb=pairs, zb=zpairs))
        subs[-1]["feeds_mixer"] = kind == "ffn" and j == 0
        units += rounds * ROUND + kz
        in_rounds += rounds
        silus += rounds if kind == "ffn" else 0
        mixed += 0 if kind == "ffn" else TOKS * rounds
        pairs += n_pairs
        zpairs += kz // 2
    RG, GM = subs[1], subs[4]

    def out_base(s):
        return s["ub"] + s["rounds"] * ROUND

    def y_bank(s, t):
        if t == 1:
            return 6
        return 2 if (s["rounds"] - 1) % 2 == 0 else 0

    def mod_bank(s):
        return 2 - y_bank(s, 0)

    def cols_bank(m):
        return 4 if m >= 1 else 0

    def turn_bank(n, t):
        return 6 if (n, t) == (0, 1) else 4

    AHEAD = 4
    NEXT_AT = {KF - 12: 0, KF - 8: 1, KF - 4: 2, KF - 1: 3}
    assert len(NEXT_AT) == AHEAD
    MOD_AT = {"ffn": 4, "rg": 7, "gm": 6}
    X_TURN_AT = {"ffn": KF - 4, "rg": KD - 4, "gm": D_G // P - 4}

    ada_v = ada_w.rearrange("l (p k) (b c) -> l k b p c", p=P, c=D)
    adab_v = ada_b.rearrange("l (b c) -> l b c", c=D)
    ffn_in_v = ffn_w_in.rearrange("l s (p k) (g n c) -> l s n p (k g) c", p=P, g=2, c=HALF // 2)
    ffn_out_v = ffn_w_out.rearrange("l s (k p) n -> l s k p n", p=P)
    rg_in_v = rg_w_in.rearrange("l (p k) (n c) -> l n p k c", p=P, c=HALF)
    gm_in_v = gm_w_in.rearrange("l (p k) (n c) -> l n p k c", p=P, c=HALF)
    rg_out_v = rg_w_out.rearrange("l (k p) n -> l k p n", p=P)
    gm_out_v = gm_w_out.rearrange("l (k p) n -> l k p n", p=P)

    ROW_CW = 0
    ROW_CB = ROW_CW + CONV * KD
    ROW_BA, ROW_BX, ROW_LAM, ROW_BS = ROW_CB + KD, ROW_CB + 2 * KD, ROW_CB + 3 * KD, ROW_CB + 4 * KD
    ROWS = ROW_BS + GROUPS

    ctx = ExitStack()
    with ctx:
        def sb(name, shape, dt=F32):
            return ctx.enter_context(nc.sbuf_tensor(name, shape, dt))

        def under(name, shape):
            with nc.sbuf_tensor(name, shape, F32) as t:
                return t

        def sem(name):
            return ctx.enter_context(nc.semaphore(name))

        xres = sb("xres", [P, TOKS, D])
        h_hi = sb("h_hi", [P, KD, SEQ], F32R)
        h_lo = sb("h_lo", [P, KD, SEQ], F32R)
        z_hi_f32 = under("z_hi_f32", [P, KF, SEQ])
        z_hi = sb("z_hi", [P, KF, SEQ], F32R)
        z_lo_f32 = under("z_lo_f32", [P, KF, SEQ])
        z_lo = sb("z_lo", [P, KF, SEQ], F32R)
        w_hi = sb("w_hi", [P, SLOTS, UNIT], F32R)
        w_raw = under("w_raw", [P, SLOTS, UNIT])
        w_lo = sb("w_lo", [P, SLOTS, UNIT], F32R)
        ada_raw = sb("ada_raw", [P, 3, D])
        ada_acc = sb("ada_acc", [P, 3, D])
        gate_sc = sb("gate_sc", [P, D])
        stage = sb("stage", [P, 2, TOKS, HALF])
        MIX = max(HEADS * (SEQ + CONV - 1) + 2 * HEADS * SEQ, 2 * TOKS * D_G)
        mix = sb("mix", [P, MIX])
        squares = sb("squares", [P, HALF], mybir.dt.bfloat16)
        pre_g = sb("pre_g", [P, NSUBL, KD])
        prm = sb("prm", [P, ROWS])
        ident = sb("ident", [P, P])
        ones = sb("ones", [P, P])
        c_in = sb("c_in", [P, KD])
        c_act = sb("c_act", [P, KD, 1])
        mod_a = sb("mod_a", [P, KD])
        mod_b = sb("mod_b", [P, KD])
        sumsq = sb("sumsq", [P, 4, 2])
        rms = sb("rms", [P, 4])
        msq = sb("msq", [P, 4])
        neg_half = sb("neg_half", [P, 1])
        bn = sb("bn", [P, TOKS, 4, 6])
        ln_mv = sb("ln_mv", [P, TOKS, 2])
        ln_ve = sb("ln_ve", [P, TOKS])
        ln_r = sb("ln_r", [P, TOKS])
        sp = sb("sp", [P, 9, KD])
        LAM_E, LAM_W, LAM_W2, LAM_Q, LAM_T, SP_P, SP_N, HBA, HBX = range(9)

        xb_pad = mix[:, 0:HEADS * (SEQ + CONV - 1)].rearrange("p (h t) -> p h t", h=HEADS)
        o0 = HEADS * (SEQ + CONV - 1)
        HS = HEADS * SEQ
        rg_m = mix[:, 0:HS].rearrange("p (h t) -> p h t", h=HEADS)
        rg_x = mix[:, o0:o0 + HS].rearrange("p (h t) -> p h t", h=HEADS)
        rg_a = mix[:, o0 + HS:o0 + 2 * HS].rearrange("p (h t) -> p h t", h=HEADS)
        rg_a2 = mix[:, o0 + 2 * HS:o0 + 2 * HS + HS // 2].rearrange("p (h t) -> p h t", h=HEADS // 2)
        gm_v = mix[:, 0:TOKS * D_G].rearrange("p (t n) -> p t n", t=TOKS)
        gm_lg = mix[:, TOKS * D_G:(TOKS + 1) * D_G]
        gm_lb = mix[:, (TOKS + 1) * D_G:(TOKS + 2) * D_G]
        y_gated = stage[:, 0, :, :]
        xn_stage = stage[:, 0, :, :].rearrange("p a b -> p (a b)")
        h_stage = stage[:, 1, :, :].rearrange("p a (k t) -> p (a k) t", t=P)
        prm_rows = z_hi_f32[0:ROWS, KF - 1, 0:P]
        gate_w = z_lo_f32[:, KD:2 * KD, :].rearrange("p (g h) (a e) -> p g (h a) e", g=2, a=2)
        gate_t = z_hi_f32[:, KD:2 * KD, :]
        KG = D_G // P
        ws_rows = z_hi_f32[:, KG:KG + 4, :].rearrange("p g (a t) -> p (g a) t", a=2)
        ws_t = z_lo_f32[:, KG:KG + 4, :].rearrange("p g (a t) -> p (g a) t", a=2)
        LAND = 8
        land = mix[:, 0:LAND * D].rearrange("p (s c) -> p s c", s=LAND)

        def pair_of(z, n, it=0, per=0):
            return z[:].rearrange("p (n k) t -> p n k t", k=2)[:, it * per + n]

        ps = ctx.enter_context(nc.psum_tensor("ps", [P, 8, HALF], F32))

        raw_landed = [sem(f"raw_landed{n}") for n in range(SLOTS)]
        hi_done, lo_done = sem("hi_done"), sem("lo_done")
        unit_used = sem("unit_used")
        in_ready = sem("in_ready")
        silu_done, z_staged = sem("silu_done"), sem("z_staged")
        mix_staged = sem("mix_staged")
        u_staged = sem("u_staged")
        pair_done = sem("pair_done")
        zhi_done, z_ready = sem("zhi_done"), sem("z_ready")
        rg_pair_read = sem("rg_pair_read")
        y_ready = sem("y_ready")
        y_sq, y_rms = sem("y_sq"), sem("y_rms")
        y_scaled, x_new = sem("y_scaled"), sem("x_new")
        x_sq, x_rms, x_normed = sem("x_sq"), sem("x_rms"), sem("x_normed")
        x_turned = sem("x_turned")
        h_full = [sem(f"h_full{g}") for g in range(2)]
        hhi_done, h_ready = sem("hhi_done"), sem("h_ready")
        ada_landed = [sem(f"ada_landed{q}") for q in range(3)]
        ada_added = sem("ada_added")
        land_full = [sem(f"land_full{n}") for n in range(LAND)]
        land_added = sem("land_added")
        acc_zero, acc_bias = sem("acc_zero"), sem("acc_bias")
        gate_summed, cols_summed = sem("gate_summed"), sem("cols_summed")
        gate_set, mod_set = sem("gate_set"), sem("mod_set")
        post_landed = sem("post_landed")
        c_landed, prm_landed, x_landed, ws_landed = (sem("c_landed"), sem("prm_landed"), sem("x_landed"),
                                                     sem("ws_landed"))
        pre_landed = sem("pre_landed")
        prm_turned, prm_done, c_done = sem("prm_turned"), sem("prm_done"), sem("c_done")
        lam_abs, lam_exp = sem("lam_abs"), sem("lam_exp")
        consts = sem("consts")
        pool_step = sem("pool_step")
        dve_step = sem("dve_step")
        tr_done = sem("tr_done")
        ws_turned, ws_copied, ws_masked = sem("ws_turned"), sem("ws_copied"), sem("ws_masked")
        gate_w_landed = sem("gate_w_landed")
        pads = sem("pads")
        conv_done, gates_done, gates_read = sem("conv_done"), sem("gates_done"), sem("gates_read")
        tan_done, exp_done = sem("tan_done"), sem("exp_done")
        a2_done = sem("a2_done")
        m2_done, mult_done, hs_done = sem("m2_done"), sem("mult_done"), sem("hs_done")
        ln_landed, ln_var, ln_rstd, v_normed = (sem("ln_landed"), sem("ln_var"), sem("ln_rstd"),
                                                sem("v_normed"))
        sp_done, sp_read = sem("sp_done"), sem("sp_read")
        out_landed = sem("out_landed")

        block = ctx.enter_context(nc.Block())

        @block.sync
        def _(sync):
            def unit(u, src, n=0, runs=1):
                s = u % SLOTS
                if u >= SLOTS:
                    sync.wait_ge(unit_used, u - SLOTS + 1 + n)
                d = w_raw[:, s, :]
                if runs > 1:
                    d = d.rearrange("p (k c) -> p k c", k=runs)
                sync.dma_start(d, src).then_inc(raw_landed[s], 16)

            def ffn_round(s, r, it=0, per=0):
                v = ffn_in_v[s["l"], s["j"] // 2]
                for q in range(ROUND):
                    unit(s["ub"] + r * ROUND + q, v[it * per + r, :, 4 * q:4 * q + 4, :],
                         n=it * (per * ROUND), runs=4)

            def mixer_round(s, r):
                v = (rg_in_v if s["kind"] == "rg" else gm_in_v)[s["l"] // 2]
                col = r if s["kind"] == "rg" else (r + s["rounds"] // 2) % s["rounds"]
                for q in range(ROUND):
                    unit(s["ub"] + r * ROUND + q, v[col, :, 2 * q:2 * q + 2, :], runs=2)

            sync.dma_start(c_in[:], c.rearrange("b (p k) -> p (b k)", p=P)).then_inc(c_landed, 16)
            for n in range(2 * KD):
                q, k = divmod(n, KD)
                if n >= LAND:
                    sync.wait_ge(land_added, n - LAND + 1)
                sync.dma_start(land[:, n % LAND, :], ada_v[0, k, 1 - q]).then_inc(land_full[n % LAND], 16)

            for s in subs:
                i, kind, R = s["i"], s["kind"], s["rounds"]
                if kind == "ffn":
                    for r in range(HEAD):
                        ffn_round(s, r)
                    with sync.Fori(0, (R - HEAD) // 2) as it:
                        ffn_round(s, HEAD, it, 2)
                        ffn_round(s, HEAD + 1, it, 2)
                    ffn_round(s, R - 1)
                else:
                    for r in range(R):
                        mixer_round(s, r)
                wv = {"ffn": ffn_out_v[s["l"], s["j"] // 2], "rg": rg_out_v[0], "gm": gm_out_v[0]}[kind]
                ob, loops = out_base(s), s["kz"] // SLOTS
                with sync.Fori(0, loops) as it:
                    for o in range(SLOTS):
                        unit(ob + o, wv[it * SLOTS + o], n=it * SLOTS)
                for o in range(loops * SLOTS, s["kz"]):
                    unit(ob + o, wv[o])

            for t in range(TOKS):
                for g in range(2):
                    cols = slice(g * HALF, (g + 1) * HALF)
                    sync.wait_ge(x_new, 4 * (NSUBL - 1) + 2 * t + g + 1)
                    sync.dma_start(out[0, t * P:(t + 1) * P, cols], xres[:, t, cols]).then_inc(out_landed, 16)
            sync.wait_ge(out_landed, 32 * TOKS)

        @block.gpsimd
        def _(pool):
            steps = [0]

            def link(ins):
                steps[0] += 1
                ins.then_inc(pool_step, 1)
                pool.wait_ge(pool_step, steps[0])

            def acc_init(m):
                lo, hi = (1, 3) if m == 0 else ((0, 1) if m == NSUBL else (0, 3))
                if m >= 1:
                    pool.wait_ge(cols_summed, m)
                nc.gpsimd.memset(ada_acc[:, lo:hi, :], 0.0).then_inc(acc_zero, 1)
                pool.wait_ge(acc_zero, m + 1)
                if m >= 1:
                    l, j = divmod(m - 1, N_SUB)
                    pool.dma_start(ada_acc[0:1, 0, :], adab_v[l, 3 * j + 2:3 * j + 3, :]).then_inc(acc_bias, 16)
                if m < NSUBL:
                    l, j = divmod(m, N_SUB)
                    pool.dma_start(ada_acc[0:1, 1:3, :], adab_v[l:l + 1, 3 * j:3 * j + 2, :]).then_inc(acc_bias, 16)

            def ada_load(i, k, it=0):
                l, j = divmod(i, N_SUB)
                l2, j2 = divmod(i + 1, N_SUB)
                blocks = [(l, 3 * j + 2)] + ([(l2, 3 * j2), (l2, 3 * j2 + 1)] if i + 1 < NSUBL else [])
                for q, (lq, b) in enumerate(blocks):
                    if k >= 1:
                        pool.wait_ge(ada_added, 3 * i * KD + len(blocks) * (k - 1) + q + 1 + it * len(blocks))
                    elif i >= 1:
                        pool.wait_ge(ada_added, 3 * (i * KD - 1) + q + 1)
                    pool.dma_start(ada_raw[:, q, :], ada_v[lq, it + k, b]).then_inc(ada_landed[q], 16)

            def next_set(i):
                if i < NSUBL:
                    ada_load(i, 0)
                    acc_init(i + 1)

            def inv_rms(q, wait, n, signal):
                pool.wait_ge(wait, n)
                link(nc.gpsimd.tensor_scalar(msq[:, q:q + 1], sumsq[:, q, 0:1], EPS, sumsq[:, q, 1:2],
                                             ALU.add, ALU.add))
                nc.gpsimd.tensor_tensor(rms[:, q:q + 1], msq[:, q:q + 1], neg_half[:], ALU.pow).then_inc(signal, 1)

            nc.gpsimd.memset(ada_acc[:, 1:3, :], 0.0).then_inc(acc_zero, 1)
            pool.wait_ge(acc_zero, 1)
            pool.dma_start(ada_acc[0:1, 1:3, :], adab_v[0:1, 0:2, :]).then_inc(acc_bias, 16)
            link(nc.gpsimd.memset(ident[:], 0.0))
            nc.gpsimd.memset(ones[:], 1.0).then_inc(consts, 1)
            nc.gpsimd.memset(neg_half[:], -0.5).then_inc(consts, 1)
            nc.gpsimd.affine_select(out=ident[:], in_=ident[:], compare_op=ALU.not_equal, fill=1.0, base=0,
                                    pattern=[[-1, P]], channel_multiplier=1).then_inc(consts, 1)
            pool.wait_ge(consts, 3)
            for t in range(TOKS):
                inv_rms(2 + t, x_sq, 2 * t + 2, x_rms)
            acc_init(1)

            for s in subs:
                i = s["i"]
                if i >= 1:
                    pool.wait_ge(x_new, 4 * i)
                pool.dma_start(gate_sc[:], norm_post[s["l"], s["j"]].partition_broadcast(P)).then_inc(post_landed, 16)
                if s["kind"] == "rg":
                    nc.gpsimd.memset(xb_pad[:, :, 0:CONV - 1], 0.0).then_inc(pads, 1)
                    pool.dma_start(gate_w[:, 0], rg_w_a[0].rearrange("h d e -> d h e")).then_inc(gate_w_landed, 16)
                    pool.dma_start(gate_w[:, 1], rg_w_x[0].rearrange("h d e -> d h e")).then_inc(gate_w_landed, 16)
                if s["kind"] == "gm":
                    pool.dma_start(ws_rows, gm_w_s[0].rearrange("g t s -> t g s")).then_inc(ws_landed, 16)
                first = AHEAD if i > 0 and subs[i - 1]["feeds_mixer"] else 1
                if i == 0:
                    ada_load(i, 0)
                if s["kind"] == "gm":
                    ada_load(i, first)
                    ada_load(i, first + 1)
                    pool.dma_start(gm_lg, gm_ln_g[0].partition_broadcast(P)).then_inc(ln_landed, 16)
                    pool.dma_start(gm_lb, gm_ln_b[0].partition_broadcast(P)).then_inc(ln_landed, 16)
                    ada_load(i, first + 2)
                else:
                    with pool.Fori(0, KD - first) as it:
                        ada_load(i, first, it)
                if s["kind"] == "gm":
                    pool.wait_ge(ws_copied, 2)
                    nc.gpsimd.affine_select(out=ws_t, in_=ws_t, compare_op=ALU.is_ge, fill=0.0, base=0,
                                            pattern=[[0, GROUPS], [1, P]], channel_multiplier=-1).then_inc(ws_masked, 1)
                    for t in range(TOKS):
                        pool.wait_ge(ln_var, t + 1)
                        link(nc.gpsimd.tensor_scalar(ln_ve[:, t:t + 1], ln_mv[:, t, 1:2], EPS, None, ALU.add))
                        nc.gpsimd.tensor_tensor(ln_r[:, t:t + 1], ln_ve[:, t:t + 1], neg_half[:],
                                                ALU.pow).then_inc(ln_rstd, 1)
                    ada_load(i, first + 3)
                if s["kind"] != "rg":
                    next_set(i + 1)
                if s["feeds_mixer"]:
                    for k in range(1, AHEAD):
                        ada_load(i + 1, k)
                for t in range(TOKS):
                    inv_rms(t, y_sq, 4 * i + 2 * t + 2, y_rms)
                    if i + 1 < NSUBL:
                        inv_rms(2 + t, x_sq, 4 * (i + 1) + 2 * t + 2, x_rms)
                if s["kind"] == "rg":
                    next_set(i + 1)

        @block.scalar
        def _(act):
            def hi(u, n=0):
                s = u % SLOTS
                act.wait_ge(raw_landed[s], 16 * (u // SLOTS + 1) + n * (16 // SLOTS))
                nc.scalar.activation(w_hi[:, s, :], w_raw[:, s, :], ACT.Copy).then_inc(hi_done, 1)

            def round_ready(s, r, t, it=0, per=0):
                if t == 0:
                    act.wait_ge(in_ready, s["rb"] + r + 1 + it * per)
                else:
                    act.wait_ge(unit_used, s["ub"] + (r + 1) * ROUND + it * (per * ROUND))

            def silu(s, r, t, it=0, per=0):
                round_ready(s, r, t, it, per)
                p = r % 2
                nc.scalar.activation(stage[:, p, t, 0:HALF // 2], ps[:, 2 * p + t, 0:HALF // 2],
                                     ACT.Silu).then_inc(silu_done, 1)

            def pair_hi(s, n, it=0, per=0):
                act.wait_ge(pair_done, s["tb"] + n + 1 + it * per)
                b = 4 + n % 2
                src = ps[:, b, :].rearrange("p (k t) -> p k t", k=2)
                nc.scalar.activation(pair_of(z_hi, n, it, per), src, ACT.Copy).then_inc(zhi_done, 1)

            before = []

            def mean_square(src, q, g, signal, n):
                if before:
                    act.wait_ge(*before[-1])
                before[:] = [(signal, n)]
                nc.scalar.activation(squares[:], src, ACT.Square, scale=float(D) ** -0.5,
                                     accum_out=sumsq[:, q, g:g + 1]).then_inc(signal, 1)

            def y_square(s, t):
                if t == 0:
                    act.wait_ge(y_ready, s["i"] + 1)
                else:
                    act.wait_ge(unit_used, out_base(s) + s["kz"])
                for g in range(2):
                    if g == 1:
                        act.wait_ge(y_scaled, 4 * s["i"] + 2 * t + 1)
                    mean_square(ps[:, y_bank(s, t) + g, :], t, g, y_sq, 4 * s["i"] + 2 * t + g + 1)

            def x_square(n, t):
                if n == 0:
                    act.wait_ge(x_landed, 16)
                for g in range(2):
                    if n >= 1:
                        act.wait_ge(x_new, 4 * (n - 1) + 2 * t + g + 1)
                    mean_square(xres[:, t, g * HALF:(g + 1) * HALF], 2 + t, g, x_sq, 4 * n + 2 * t + g + 1)

            def h_part(n, t):
                act.wait_ge(x_turned, 2 * (2 * n + t) + 2)
                act.wait_ge(mod_set, n + 1)
                if (n, t) == (0, 1):
                    act.wait_ge(h_ready, 2)
                for k in range(4, 8):
                    last = nc.scalar.activation(h_stage[:, k, :], ps[:, turn_bank(n, t) + 1, (k % 4) * P:(k % 4 + 1) * P],
                                                ACT.Identity, scale=mod_a[:, k:k + 1], bias=mod_b[:, k:k + 1])
                last.then_inc(h_full[1], 1)
                for g in range(2):
                    act.wait_ge(h_full[g], 2 * n + t + 1)
                    nc.scalar.activation(h_hi[:, 4 * g:4 * g + 4, t * P:(t + 1) * P], h_stage[:, 4 * g:4 * g + 4, :],
                                         ACT.Copy).then_inc(hhi_done, 1)

            act.dma_start(xres[:], x[0].rearrange("(t p) d -> p t d", p=P)).then_inc(x_landed, 16)
            act.dma_start(pre_g[:], norm_pre.rearrange("l j (p k) -> p (l j) k", p=P)).then_inc(pre_landed, 16)
            for row, src in ((ROW_CW, rg_conv_w.rearrange("l w (k p) -> (l w k) p", p=P)),
                             (ROW_CB, rg_conv_b.rearrange("l (k p) -> (l k) p", p=P)),
                             (ROW_BA, rg_b_a.rearrange("l (k p) -> (l k) p", p=P)),
                             (ROW_BX, rg_b_x.rearrange("l (k p) -> (l k) p", p=P)),
                             (ROW_LAM, rg_lambda.rearrange("l (k p) -> (l k) p", p=P)),
                             (ROW_BS, gm_b_s.rearrange("l g t -> (l g) t"))):
                act.dma_start(prm_rows[row:row + src.shape[0], :], src).then_inc(prm_landed, 16)

            act.wait_ge(c_landed, 16)
            nc.scalar.activation(c_act[:, :, 0], c_in[:], ACT.Silu).then_inc(c_done, 1)
            for t in range(TOKS):
                x_square(0, t)
            act.wait_ge(lam_abs, 1)
            nc.scalar.activation(sp[:, LAM_E, :], sp[:, LAM_T, :], ACT.Exp, scale=-1.0).then_inc(lam_exp, 1)
            hi(0)
            hi(1)
            h_part(0, 0)
            hi(2)
            hi(3)
            h_part(0, 1)
            for u in range(4, SLOTS):
                hi(u)

            for s in subs:
                i, kind, ub, ob, R = s["i"], s["kind"], s["ub"], out_base(s), s["rounds"]
                act.wait_ge(h_ready, 4 * i + 4)
                if kind == "ffn":
                    for t in range(TOKS):
                        silu(s, 0, t)
                    for q in range(4):
                        if q == 3:
                            pair_hi(s, 0)
                        hi(ub + 8 + q)
                    with act.Fori(0, (R - HEAD) // 2) as it:
                        for r in (2, 3):
                            for t in range(TOKS):
                                silu(s, r - 1, t, it, 2)
                            for q in range(4):
                                if q == 3:
                                    pair_hi(s, r - 1, it, 2)
                                hi(ub + 4 * r + 4 + q, n=it * 8)
                    for r in (R - 1, R):
                        for t in range(TOKS):
                            silu(s, r - 1, t)
                        for q in range(4):
                            if q == 3:
                                pair_hi(s, r - 1)
                            hi(ub + 4 * r + 4 + q)
                elif kind == "rg":
                    def stage_round(r, f):
                        for t in range(TOKS):
                            round_ready(s, r, t)
                            nc.scalar.activation(stage[:, r % 2, t, :], ps[:, 2 * (r % 2) + t, :],
                                                 f).then_inc(mix_staged, 1)

                    def take_pair(n):
                        act.wait_ge(pair_done, s["tb"] + n + 1)
                        src = ps[:, 4 + n % 2, :].rearrange("p (k t) -> p k t", k=2)
                        if n == 0:
                            act.wait_ge(pads, 1)
                        nc.scalar.activation(xb_pad[:, 2 * n:2 * n + 2, CONV - 1:], src, ACT.Copy)
                        for h in (2 * n, 2 * n + 1):
                            w = ROW_CW + (CONV - 1) * KD + h
                            last = nc.scalar.activation(rg_x[:, h, :], src[:, h % 2, :], ACT.Identity,
                                                        scale=prm[:, w:w + 1], bias=prm[:, ROW_CB + h:ROW_CB + h + 1])
                        last.then_inc(rg_pair_read, 1)

                    def gate_tanh(h):
                        act.wait_ge(gates_done, h + 1)
                        b = 6 + h % 2
                        nc.scalar.activation(rg_a[:, h, :], ps[:, b, 0:SEQ], ACT.Tanh, scale=0.5,
                                             bias=sp[:, HBA, h:h + 1]).then_inc(tr_done, 1)
                        nc.scalar.activation(gate_t[:, h, :], ps[:, b, SEQ:2 * SEQ], ACT.Tanh, scale=0.5,
                                             bias=sp[:, HBX, h:h + 1]).then_inc(gates_read, 1)

                    def decay(h):
                        act.wait_ge(tr_done, h + 1)
                        nc.scalar.activation(rg_m[:, h, :], rg_a[:, h, :], ACT.Tanh, scale=sp[:, SP_P, h:h + 1],
                                             bias=sp[:, SP_P, h:h + 1]).then_inc(tan_done, 1)
                        act.wait_ge(tan_done, h + 1)
                        nc.scalar.activation(rg_a[:, h, :], rg_a[:, h, :], ACT.Exp, scale=sp[:, SP_N, h:h + 1],
                                             bias=sp[:, SP_N, h:h + 1]).then_inc(exp_done, 1)

                    stage_round(0, ACT.Copy)
                    hi(ub + 8)
                    hi(ub + 9)
                    take_pair(0)
                    take_pair(1)
                    hi(ub + 10)
                    stage_round(1, ACT.Copy)
                    hi(ub + 11)
                    take_pair(2)
                    take_pair(3)
                    for h in range(HEADS):
                        hi(ub + 12 + h)
                        gate_tanh(h)
                        decay(h)
                        if h >= HEADS // 2 and h % 2 == 1:
                            act.wait_ge(exp_done, h + 1)
                            nc.scalar.activation(rg_a2[:, h - HEADS // 2 - 1:h - HEADS // 2 + 1, :],
                                                 rg_a[:, h - 1:h + 1, :], ACT.Square).then_inc(a2_done, 1)
                    for g in range(2):
                        act.wait_ge(m2_done, 4 * g + 4)
                        nc.scalar.activation(rg_m[:, 4 * g:4 * g + 4, :], rg_m[:, 4 * g:4 * g + 4, :], ACT.Sqrt,
                                             scale=0.25).then_inc(mult_done, 1)
                    for r in (2, 3):
                        stage_round(r, ACT.Gelu_apprx_tanh)
                    for n in range(KD // 2):
                        act.wait_ge(hs_done, n + 1)
                        nc.scalar.activation(z_hi[:, 2 * n:2 * n + 2, :], rg_x[:, 2 * n:2 * n + 2, :],
                                             ACT.Copy).then_inc(zhi_done, 1)
                    for q in range(4):
                        hi(ob + 4 + q)
                else:
                    def gelu_v(r):
                        for t in range(TOKS):
                            round_ready(s, r, t)
                            nc.scalar.activation(gm_v[:, t, r * HALF:(r + 1) * HALF], ps[:, 2 * (r % 2) + t, :],
                                                 ACT.Gelu_apprx_tanh).then_inc(mix_staged, 1)

                    def gelu_u(r):
                        for t in range(TOKS):
                            round_ready(s, r, t)
                            nc.scalar.activation(stage[:, r % 2, t, :], ps[:, 2 * (r % 2) + t, :],
                                                 ACT.Gelu_apprx_tanh).then_inc(mix_staged, 1)

                    def hi4(r, pairs_at=None):
                        for q in range(4):
                            if q == 3 and pairs_at is not None:
                                pair_hi(s, pairs_at)
                                pair_hi(s, pairs_at + 1)
                            hi(ub + 4 * r + 4 + q)

                    for r in range(1, 5):
                        gelu_v(r - 1)
                        hi4(r)
                    gelu_u(4)
                    hi4(5)
                    for n in range(TOKS * GROUPS // 2):
                        t, g2 = divmod(n, GROUPS // 2)
                        act.wait_ge(sp_done, n + 1)
                        for g in (2 * g2, 2 * g2 + 1):
                            last = nc.scalar.activation(gm_v[:, t, g * GD:(g + 1) * GD],
                                                        ps[:, 6 + n % 2, (g % 2) * GD:(g % 2) * GD + GD],
                                                        ACT.Identity, bias=prm[:, ROW_BS + g:ROW_BS + g + 1])
                        last.then_inc(sp_read, 1)
                    gelu_u(5)
                    hi4(6, 0)
                    gelu_u(6)
                    hi4(7, 2)
                    gelu_u(7)
                    hi(ob + 4)
                    hi(ob + 5)
                    pair_hi(s, 4)
                    pair_hi(s, 5)
                    hi(ob + 6)
                    hi(ob + 7)
                    pair_hi(s, 6)
                    pair_hi(s, 7)

                for o in range(SLOTS, s["kz"]):
                    hi(ob + o)
                nxt = ob + s["kz"]
                y_square(s, 0)
                if i + 1 < NSUBL:
                    x_square(i + 1, 0)
                    hi(nxt)
                    hi(nxt + 1)
                    h_part(i + 1, 0)
                    hi(nxt + 2)
                    y_square(s, 1)
                    hi(nxt + 3)
                    x_square(i + 1, 1)
                    hi(nxt + 4)
                    hi(nxt + 5)
                    h_part(i + 1, 1)
                    hi(nxt + 6)
                    hi(nxt + 7)
                else:
                    y_square(s, 1)

        @block.vector
        def _(dve):
            steps = [0]

            def link(ins):
                steps[0] += 1
                ins.then_inc(dve_step, 1)
                dve.wait_ge(dve_step, steps[0])

            def lo(u, n=0):
                s = u % SLOTS
                dve.wait_ge(hi_done, u + 1 + n)
                nc.vector.tensor_tensor(w_lo[:, s, :], w_raw[:, s, :], w_hi[:, s, :].bitcast(F32),
                                        ALU.subtract).then_inc(lo_done, 1)

            def ada(i, k, it=0):
                n = 3 if i + 1 < NSUBL else 1
                if k == 0:
                    dve.wait_ge(acc_bias, 16 * (1 + 2 * i + (2 if i + 1 < NSUBL else 1)))
                for q in range(n):
                    dve.wait_ge(ada_landed[q], 16 * (i * KD + k + 1) + it * 16)
                    if k >= 1:
                        dve.wait_ge(ada_added, 3 * i * KD + n * (k - 1) + q + 1 + it * n)
                    nc.vector.scalar_tensor_tensor(out=ada_acc[:, q, :], in0=ada_raw[:, q, :],
                                                   scalar=c_act[:, it + k, :], in1=ada_acc[:, q, :],
                                                   op0=ALU.mult, op1=ALU.add).then_inc(ada_added, 1)

            def gate_up(s, r, t, it=0, per=0):
                dve.wait_ge(silu_done, 2 * (s["sb"] + r) + t + 1 + it * (2 * per))
                p = r % 2
                nc.vector.tensor_tensor(stage[:, p, t, HALF // 2:], ps[:, 2 * p + t, HALF // 2:],
                                        stage[:, p, t, 0:HALF // 2], ALU.mult).then_inc(z_staged, 1)

            def pair_lo(s, n, it=0, per=0):
                dve.wait_ge(zhi_done, s["zb"] + n + 1 + it * per)
                src = ps[:, 4 + n % 2, :].rearrange("p (k t) -> p k t", k=2)
                nc.vector.tensor_tensor(pair_of(z_lo, n, it, per), src, pair_of(z_hi, n, it, per).bitcast(F32),
                                        ALU.subtract).then_inc(z_ready, 1)

            def y_gate(s, t):
                dve.wait_ge(gate_set, s["i"] + 1)
                if t == 0:
                    dve.wait_ge(y_ready, s["i"] + 1)
                else:
                    dve.wait_ge(unit_used, out_base(s) + s["kz"])
                    if s["i"] + 1 < NSUBL:
                        dve.wait_ge(x_turned, 4 * (s["i"] + 1) + 2)
                    else:
                        dve.wait_ge(x_new, 4 * s["i"] + 2)
                for g in (1, 0):
                    if g == 0:
                        dve.wait_ge(y_sq, 4 * s["i"] + 2 * t + 1)
                    nc.vector.tensor_tensor(y_gated[:, g, :], ps[:, y_bank(s, t) + g, :],
                                            gate_sc[:, g * HALF:(g + 1) * HALF], ALU.mult).then_inc(y_scaled, 1)

            def x_add(s, t):
                dve.wait_ge(y_rms, 2 * s["i"] + t + 1)
                dve.wait_ge(y_scaled, 4 * s["i"] + 2 * t + 2)
                for g in range(2):
                    xg = xres[:, t, g * HALF:(g + 1) * HALF]
                    nc.vector.scalar_tensor_tensor(out=xg, in0=y_gated[:, g, :], scalar=rms[:, t:t + 1], in1=xg,
                                                   op0=ALU.mult, op1=ALU.add).then_inc(x_new, 1)

            def normed(n, t):
                dve.wait_ge(x_rms, 2 * n + t + 1)
                if n == 0 and t == 1:
                    dve.wait_ge(x_turned, 2)
                nc.vector.tensor_scalar(xn_stage, xres[:, t, :], rms[:, 2 + t:3 + t], None,
                                        ALU.mult).then_inc(x_normed, 1)

            def modulated(n, t):
                dve.wait_ge(x_turned, 2 * (2 * n + t) + 1)
                dve.wait_ge(mod_set, n + 1)
                if (n, t) == (0, 1):
                    dve.wait_ge(h_ready, 2)
                for k in range(4):
                    last = nc.vector.tensor_scalar(h_stage[:, k, :], ps[:, turn_bank(n, t), k * P:(k + 1) * P],
                                                   mod_a[:, k:k + 1], mod_b[:, k:k + 1], ALU.mult, ALU.add)
                last.then_inc(h_full[0], 1)

            def h_lo_halves(n, t):
                for g in range(2):
                    dve.wait_ge(hhi_done, 2 * (2 * n + t) + g + 1)
                    sl = (slice(None), slice(4 * g, 4 * g + 4), slice(t * P, (t + 1) * P))
                    nc.vector.tensor_tensor(h_lo[sl], h_stage[:, 4 * g:4 * g + 4, :], h_hi[sl].bitcast(F32),
                                            ALU.subtract).then_inc(h_ready, 1)

            def take_gate(s):
                dve.wait_ge(gate_summed, s["i"] + 1)
                dve.wait_ge(post_landed, 16 * (s["i"] + 1))
                b = mod_bank(s)
                nc.vector.scalar_tensor_tensor(out=gate_sc[:].rearrange("p (a b) -> p a b", a=2),
                                               in0=ps[:, b:b + 2, :], scalar=float(s["res"]),
                                               in1=gate_sc[:].rearrange("p (a b) -> p a b", a=2),
                                               op0=ALU.mult, op1=ALU.mult).then_inc(gate_set, 1)

            def take_columns(m):
                dve.wait_ge(cols_summed, m + 1)
                if m == 0:
                    dve.wait_ge(pre_landed, 16)
                b = cols_bank(m)
                nc.vector.tensor_copy(mod_b[:], ps[:, b, 0:KD])
                nc.vector.scalar_tensor_tensor(out=mod_a[:], in0=ps[:, b, KD:2 * KD], scalar=1.0,
                                               in1=pre_g[:, m, :], op0=ALU.add, op1=ALU.mult).then_inc(mod_set, 1)

            def take_mod(s):
                take_gate(s)
                if s["i"] + 1 < NSUBL:
                    take_columns(s["i"] + 1)

            dve.wait_ge(c_done, 1)
            dve.wait_ge(acc_bias, 16)
            for n in range(2 * KD):
                q, k = divmod(n, KD)
                dve.wait_ge(land_full[n % LAND], 16 * (n // LAND + 1))
                if k >= 1:
                    dve.wait_ge(land_added, n)
                nc.vector.scalar_tensor_tensor(out=ada_acc[:, 2 - q, :], in0=land[:, n % LAND, :],
                                               scalar=c_act[:, k, :], in1=ada_acc[:, 2 - q, :],
                                               op0=ALU.mult, op1=ALU.add).then_inc(land_added, 1)
                if n == KD - 1:
                    normed(0, 0)
                if n == KD:
                    dve.wait_ge(prm_turned, 1)
                    nc.vector.tensor_copy(prm[:], ps[:, 1, 0:ROWS]).then_inc(prm_done, 1)
                    dve.wait_ge(prm_done, 1)
                    lam = prm[:, ROW_LAM:ROW_LAM + KD]
                    link(nc.vector.tensor_scalar(sp[:, LAM_W, :], lam, -1.0, None, ALU.mult))
                    nc.vector.tensor_tensor(sp[:, LAM_T, :], lam, sp[:, LAM_W, :], ALU.max).then_inc(lam_abs, 1)
                    nc.vector.tensor_scalar(sp[:, HBA, :], prm[:, ROW_BA:ROW_BA + KD], 0.5, None, ALU.mult)
                    nc.vector.tensor_scalar(sp[:, HBX, :], prm[:, ROW_BX:ROW_BX + KD], 0.5, None, ALU.mult)
            lo(0)
            take_columns(0)
            modulated(0, 0)
            normed(0, 1)
            lo(1)
            h_lo_halves(0, 0)
            lo(2)
            modulated(0, 1)
            lo(3)
            h_lo_halves(0, 1)
            for u in range(4, SLOTS):
                lo(u)
            dve.wait_ge(lam_exp, 1)
            e, w, w2, q_, t_ = (sp[:, z, :] for z in (LAM_E, LAM_W, LAM_W2, LAM_Q, LAM_T))
            link(nc.vector.tensor_scalar(w2, e, 2.0, None, ALU.add))
            link(nc.vector.reciprocal(q_, w2))
            link(nc.vector.tensor_tensor(w, e, q_, ALU.mult))
            link(nc.vector.tensor_tensor(w2, w, w, ALU.mult))
            link(nc.vector.tensor_scalar(q_, w2, 1.0 / 15, None, ALU.mult))
            for d in (13, 11, 9, 7, 5, 3):
                link(nc.vector.scalar_tensor_tensor(out=q_, in0=q_, scalar=1.0 / d, in1=w2,
                                                    op0=ALU.add, op1=ALU.mult))
            link(nc.vector.scalar_tensor_tensor(out=w, in0=q_, scalar=1.0, in1=w, op0=ALU.add, op1=ALU.mult))
            link(nc.vector.tensor_scalar(t_, lam, -1.0, 0.0, ALU.mult, ALU.max))
            link(nc.vector.scalar_tensor_tensor(out=q_, in0=w, scalar=2.0, in1=t_, op0=ALU.mult, op1=ALU.add))
            nc.vector.tensor_scalar(sp[:, SP_P, :], q_, 4.0, None, ALU.mult)
            link(nc.vector.tensor_scalar(sp[:, SP_N, :], q_, -4.0, None, ALU.mult))

            for s in subs:
                i, kind, ub, ob, R = s["i"], s["kind"], s["ub"], out_base(s), s["rounds"]
                if kind == "ffn":
                    gate_up(s, 0, 0)
                    ada(i, 0)
                    gate_up(s, 0, 1)
                    for q in range(4):
                        if q == 3:
                            pair_lo(s, 0)
                        lo(ub + 8 + q)
                    ada(i, 1)
                    with dve.Fori(0, (R - HEAD) // 2) as it:
                        for r in (2, 3):
                            for t in range(TOKS):
                                gate_up(s, r - 1, t, it, 2)
                            for q in range(4):
                                if q == 3:
                                    pair_lo(s, r - 1, it, 2)
                                lo(ub + 4 * r + 4 + q, n=it * 8)
                            if r == 2:
                                ada(i, 2, it)
                    for r in (R - 1, R):
                        for t in range(TOKS):
                            gate_up(s, r - 1, t)
                        for q in range(4):
                            if q == 3:
                                pair_lo(s, r - 1)
                            lo(ub + 4 * r + 4 + q)
                            if r == R and q == 0:
                                ada(i, 7)
                        if r < R:
                            ada(i, 6)
                    for o in range(8, s["kz"]):
                        lo(ob + o)
                        if o == 9:
                            take_mod(s)
                        if o in NEXT_AT and s["feeds_mixer"]:
                            ada(i + 1, NEXT_AT[o])
                elif kind == "rg":
                    def conv(heads):
                        dve.wait_ge(rg_pair_read, heads[-1] // 2 + 1)
                        for k in range(CONV - 1):
                            for h in heads:
                                if k >= 1:
                                    dve.wait_ge(conv_done, conv_n[0] - len(heads) + 1)
                                w = prm[:, ROW_CW + k * KD + h:ROW_CW + k * KD + h + 1]
                                nc.vector.scalar_tensor_tensor(
                                    out=rg_x[:, h, :], in0=xb_pad[:, h, k:k + SEQ], scalar=w,
                                    in1=rg_x[:, h, :], op0=ALU.mult, op1=ALU.add).then_inc(conv_done, 1)
                                conv_n[0] += 1

                    conv_n = [0]

                    def gate_math(h):
                        hh = (slice(None), slice(h, h + 2), slice(None))
                        dve.wait_ge(gates_read, h + 2)
                        link(nc.vector.scalar_tensor_tensor(out=rg_x[hh], in0=gate_t[hh], scalar=1.0,
                                                            in1=rg_x[hh], op0=ALU.add, op1=ALU.mult))
                        if h < HEADS // 2:
                            dve.wait_ge(exp_done, h + 2)
                            link(nc.vector.tensor_tensor(gate_t[hh], rg_a[hh], rg_a[hh], ALU.mult))
                            a2 = gate_t[hh]
                        else:
                            dve.wait_ge(a2_done, h // 2 - HEADS // 4 + 1)
                            a2 = rg_a2[:, h - HEADS // 2:h - HEADS // 2 + 2, :]
                        nc.vector.scalar_tensor_tensor(out=rg_m[hh], in0=a2, scalar=1.0, in1=rg_m[hh],
                                                       op0=ALU.add, op1=ALU.mult).then_inc(m2_done, 2)

                    ada(i, 4)
                    lo(ub + 8)
                    lo(ub + 9)
                    conv(range(0, 4))
                    for q in range(10, 13):
                        lo(ub + q)
                    conv(range(4, 6))
                    lo(ub + 13)
                    conv(range(6, 8))
                    lo(ub + 14)
                    ada(i, 5)
                    for h in range(0, HEADS, 2):
                        gate_math(h)
                        if h < 6:
                            lo(ub + 15 + h // 2)
                        if h == 2:
                            ada(i, 6)
                    for g in range(2):
                        dve.wait_ge(mult_done, g + 1)
                        hs4 = (slice(None), slice(4 * g, 4 * g + 4), slice(None))
                        link(nc.vector.tensor_tensor(rg_x[hs4], rg_m[hs4], rg_x[hs4], ALU.mult))
                        for h in range(4 * g, 4 * g + 4):
                            last = nc.vector.tensor_tensor_scan(rg_m[:, h, :], rg_a[:, h, :], rg_x[:, h, :], 0.0,
                                                                ALU.mult, ALU.add)
                        link(last)

                    def hs_gated(n):
                        dve.wait_ge(pair_done, s["tb"] + KD // 2 + n + 1)
                        nc.vector.tensor_tensor(rg_x[:, 2 * n:2 * n + 2, :], rg_m[:, 2 * n:2 * n + 2, :],
                                                ps[:, 4 + n, :].rearrange("p (k t) -> p k t", k=2),
                                                ALU.mult).then_inc(hs_done, 1)

                    def hs_lo(n):
                        pr = (slice(None), slice(2 * n, 2 * n + 2), slice(None))
                        dve.wait_ge(zhi_done, s["zb"] + n + 1)
                        nc.vector.tensor_tensor(z_lo[pr], rg_x[pr], z_hi[pr].bitcast(F32),
                                                ALU.subtract).then_inc(z_ready, 1)

                    hs_gated(0)
                    hs_gated(1)
                    hs_lo(0)
                    lo(ob + 2)
                    hs_lo(1)
                    hs_gated(2)
                    lo(ob + 3)
                    hs_gated(3)
                    hs_lo(2)
                    hs_lo(3)
                    lo(ob + 4)
                    lo(ob + 5)
                    lo(ob + 6)
                    lo(ob + 7)
                    ada(i, 7)
                else:
                    def v_stats(r):
                        for t in range(TOKS):
                            dve.wait_ge(mix_staged, s["mb"] + 2 * r + t + 1)
                            nc.vector.bn_stats(bn[:, t, r, :], gm_v[:, t, r * HALF:(r + 1) * HALF]).then_inc(v_normed, 1)

                    def u_gate(r):
                        if r == 4:
                            dve.wait_ge(sp_read, TOKS * GROUPS // 2)
                        for t in range(TOKS):
                            dve.wait_ge(mix_staged, s["mb"] + 2 * r + t + 1)
                            nc.vector.tensor_tensor(stage[:, r % 2, t, :], stage[:, r % 2, t, :],
                                                    gm_v[:, t, (r - 4) * HALF:(r - 3) * HALF],
                                                    ALU.mult).then_inc(u_staged, 1)

                    def lo4(r, pairs_at=None):
                        for q in range(4):
                            if q == 3 and pairs_at is not None:
                                pair_lo(s, pairs_at)
                                pair_lo(s, pairs_at + 1)
                            lo(ub + 4 * r + 4 + q)

                    def layer_norm(t):
                        link(nc.vector.scalar_tensor_tensor(out=gm_v[:, t, :], in0=gm_v[:, t, :],
                                                            scalar=ln_mv[:, t, 0:1], in1=gm_lg,
                                                            op0=ALU.subtract, op1=ALU.mult))
                        dve.wait_ge(ln_rstd, t + 1)
                        nc.vector.scalar_tensor_tensor(out=gm_v[:, t, :], in0=gm_v[:, t, :], scalar=ln_r[:, t:t + 1],
                                                       in1=gm_lb, op0=ALU.mult, op1=ALU.add).then_inc(v_normed, 1)

                    ada(i, 4)
                    v_stats(0)
                    lo4(1)
                    for g in range(2):
                        dve.wait_ge(ws_turned, g + 1)
                        nc.vector.tensor_copy(ws_t[:, 4 * g:4 * g + 4, :],
                                              ps[:, 6 + g, :].rearrange("p (g t) -> p g t", g=4)).then_inc(ws_copied, 1)
                    v_stats(1)
                    lo4(2)
                    ada(i, 5)
                    v_stats(2)
                    lo4(3)
                    v_stats(3)
                    dve.wait_ge(v_normed, 4 * TOKS)
                    for t in range(TOKS):
                        nc.vector.bn_aggr(ln_mv[:, t, :], bn[:, t, :, :]).then_inc(ln_var, 1)
                    dve.wait_ge(ln_var, 2)
                    dve.wait_ge(ln_landed, 32)
                    lo(ub + 20)
                    layer_norm(0)
                    lo(ub + 21)
                    lo(ub + 22)
                    layer_norm(1)
                    lo(ub + 23)
                    lo4(5)
                    ada(i, 6)
                    u_gate(4)
                    u_gate(5)
                    lo4(6, 0)
                    u_gate(6)
                    lo4(7, 2)
                    u_gate(7)
                    lo(ob + 4)
                    lo(ob + 5)
                    pair_lo(s, 4)
                    pair_lo(s, 5)
                    lo(ob + 6)
                    lo(ob + 7)
                    pair_lo(s, 6)
                    pair_lo(s, 7)
                    ada(i, 7)
                    for o in range(8, s["kz"]):
                        lo(ob + o)
                        if o == 12:
                            take_mod(s)

                nxt = ob + s["kz"]
                if kind == "rg":
                    take_gate(s)
                y_gate(s, 0)
                x_add(s, 0)
                if i + 1 < NSUBL:
                    normed(i + 1, 0)
                    if kind == "rg":
                        take_columns(i + 1)
                    lo(nxt)
                    modulated(i + 1, 0)
                    lo(nxt + 1)
                    h_lo_halves(i + 1, 0)
                    y_gate(s, 1)
                    lo(nxt + 2)
                    x_add(s, 1)
                    lo(nxt + 3)
                    normed(i + 1, 1)
                    lo(nxt + 4)
                    modulated(i + 1, 1)
                    lo(nxt + 5)
                    h_lo_halves(i + 1, 1)
                    lo(nxt + 6)
                    lo(nxt + 7)
                else:
                    y_gate(s, 1)
                    x_add(s, 1)

        @block.tensor
        def _(pe):
            def three(dst, hi_, lo_, whi, wlo, start, stop):
                nc.tensor.matmul(dst, hi_, whi, start=start, stop=False)
                nc.tensor.matmul(dst, hi_, wlo, start=False, stop=False)
                return nc.tensor.matmul(dst, lo_, whi, start=False, stop=stop)

            def in_unit(u, q, p, toks, n=0):
                if 0 in toks:
                    pe.wait_ge(lo_done, u + 1 + n)
                w = u % SLOTS
                for k in (2 * q, 2 * q + 1):
                    cols = slice((k % 2) * HALF, (k % 2 + 1) * HALF)
                    for t in toks:
                        tok = slice(t * P, (t + 1) * P)
                        last = three(ps[:, 2 * p + t, :], h_hi[:, k, tok], h_lo[:, k, tok],
                                     w_hi[:, w, cols], w_lo[:, w, cols], k == 0, k == KD - 1)
                        if t == 0 and k == KD - 1:
                            last.then_inc(in_ready, 1)
                if 1 in toks:
                    last.then_inc(unit_used, 1)

            def head(s, first_turn):
                for toks, ns in (((0,), range(APART)), ((1,), range(APART)), ((0, 1), range(APART, HEAD * ROUND))):
                    for n in ns:
                        r, q = divmod(n, ROUND)
                        if s["i"] > 0 and toks == (0,) and n == TURN_AT:
                            turn_x(s["i"], 1)
                        if n in (0, 2):
                            pe.wait_ge(h_ready, 2 * (2 * s["i"] + toks[0]) + n // 2 + 1)
                        if n == HEAD * ROUND - 1:
                            first_turn()
                        in_unit(s["ub"] + n, q, r, toks)

            def turn(n, p, col0, bank=None):
                bank = 4 + n % 2 if bank is None else bank
                for t in range(TOKS):
                    for m in range(2):
                        last = nc.tensor.transpose(ps[:, bank, m * SEQ + t * P:m * SEQ + (t + 1) * P],
                                                   stage[:, p, t, col0 + m * P:col0 + (m + 1) * P], ident[:])
                last.then_inc(pair_done, 1)

            def turn_ffn(s, r, it=0, per=0):
                pe.wait_ge(z_staged, 2 * (s["sb"] + r) + 2 + it * (2 * per))
                turn(r, r % 2, HALF // 2)

            def out_unit(s, o, toks):
                u = out_base(s) + o
                if 0 in toks:
                    pe.wait_ge(lo_done, u + 1)
                    if o % 2 == 0:
                        pe.wait_ge(z_ready, s["zb"] + o // 2 + 1)
                w = u % SLOTS
                for t in toks:
                    tok = slice(t * P, (t + 1) * P)
                    for g in range(2):
                        cols = slice(g * HALF, (g + 1) * HALF)
                        last = three(ps[:, y_bank(s, t) + g, :], z_hi[:, o, tok], z_lo[:, o, tok],
                                     w_hi[:, w, cols], w_lo[:, w, cols], o == 0, o == s["kz"] - 1)
                    if t == 0 and o == s["kz"] - 1:
                        last.then_inc(y_ready, 1)
                if 1 in toks:
                    last.then_inc(unit_used, 1)

            def sum_columns(m, q):
                for k in range(KD):
                    last = nc.tensor.matmul(ps[:, cols_bank(m), (q - 1) * KD + k:(q - 1) * KD + k + 1],
                                            ada_acc[:, q, k:D:KD], ones[:, 0:1], start=True, stop=True)
                return last

            def sum_mod(m, s):
                pe.wait_ge(ada_added, 3 * KD * m if m < NSUBL else 3 * KD * (m - 1) + KD)
                for g in range(2):
                    last = nc.tensor.matmul(ps[:, mod_bank(s) + g, :], ones[:], ada_acc[:, 0, g * HALF:(g + 1) * HALF],
                                            start=True, stop=True)
                last.then_inc(gate_summed, 1)
                if m < NSUBL:
                    pe.wait_ge(z_ready, s["zb"] + s["kz"] // 2)
                    for q in (1, 2):
                        last = sum_columns(m, q)
                    last.then_inc(cols_summed, 1)

            def turn_x(n, t):
                pe.wait_ge(x_normed, 2 * n + t + 1)
                if n >= 1:
                    if t == 0:
                        pe.wait_ge(mod_set, n + 1)
                    for g in range(2):
                        pe.wait_ge(h_full[g], 2 * n + t)
                for g in range(2):
                    for k in range(4):
                        last = nc.tensor.transpose(ps[:, turn_bank(n, t) + g, k * P:(k + 1) * P],
                                                   xn_stage[:, 4 * g + k:D:KD], ident[:])
                    last.then_inc(x_turned, 1)

            pe.wait_ge(consts, 3)
            pe.wait_ge(prm_landed, 16 * 6)
            nc.tensor.transpose(ps[:, 1, 0:ROWS], prm_rows, ident[0:ROWS, 0:ROWS]).then_inc(prm_turned, 1)
            turn_x(0, 0)
            pe.wait_ge(land_added, KD)
            sum_columns(0, 2)
            pe.wait_ge(land_added, 2 * KD)
            sum_columns(0, 1).then_inc(cols_summed, 1)
            turn_x(0, 1)

            for s in subs:
                i, kind, ub, R = s["i"], s["kind"], s["ub"], s["rounds"]
                extra = {}
                if kind == "ffn":
                    head(s, lambda: turn_ffn(s, 0))
                    with pe.Fori(0, (R - HEAD) // 2) as it:
                        for r in (2, 3):
                            for q in range(ROUND):
                                if q == 3:
                                    turn_ffn(s, r - 1, it, 2)
                                in_unit(ub + 4 * r + q, q, r % 2, (0, 1), n=it * 8)
                    for q in range(ROUND):
                        if q == 3:
                            turn_ffn(s, R - 2)
                        in_unit(ub + 4 * (R - 1) + q, q, (R - 1) % 2, (0, 1))
                    extra[1] = lambda: turn_ffn(s, R - 1)
                elif kind == "rg":
                    def rg_turn(r):
                        pe.wait_ge(mix_staged, s["mb"] + 2 * r + 2)
                        for m in range(2):
                            n = 2 * r + m
                            if n >= 2:
                                pe.wait_ge(rg_pair_read, min(n - 1, KD // 2))
                            turn(n, r % 2, m * 2 * P, 4 + n % (2 if r < 2 else 4))

                    def gates(h):
                        if h == 0:
                            pe.wait_ge(gate_w_landed, 32)
                        pe.wait_ge(conv_done, 8 + h + 1 if h < 4 else 12 + 6 * (h // 2 - 2) + 4 + h % 2 + 1)
                        if h >= 2:
                            pe.wait_ge(gates_read, h - 1)
                        for g in range(2):
                            last = nc.tensor.matmul(ps[:, 6 + h % 2, g * SEQ:(g + 1) * SEQ], gate_w[:, g, h, :],
                                                    rg_x[:, h, :], start=True, stop=True)
                        last.then_inc(gates_done, 1)

                    head(s, lambda: rg_turn(0))
                    between = {(2, 1): (0,), (2, 2): (1,), (2, 3): (2,), (3, 0): (3,), (3, 1): (4, 5), (3, 2): (6,),
                               (3, 3): (7,)}
                    for r in range(HEAD, R):
                        pe.wait_ge(mix_staged, s["mb"] + 2 * (r - 2) + 2)
                        for q in range(ROUND):
                            if (r, q) == (2, 1):
                                rg_turn(1)
                            for h in between.get((r, q), ()):
                                gates(h)
                            in_unit(ub + 4 * r + q, q, r % 2, (0, 1))
                    rg_turn(2)
                    pe.wait_ge(gates_read, HEADS)
                    rg_turn(3)
                else:
                    def turn_ws():
                        pe.wait_ge(ws_landed, 16)
                        for g in range(GROUPS):
                            last = nc.tensor.transpose(ps[:, 6 + g // 4, (g % 4) * P:(g % 4 + 1) * P],
                                                       ws_rows[:, g, :], ident[:])
                            if g % 4 == 3:
                                last.then_inc(ws_turned, 1)

                    def gm_turn(r):
                        pe.wait_ge(u_staged, 2 * (r - 4) + 2)
                        for m in range(2):
                            n = 2 * (r - 4) + m
                            if n >= 2:
                                pe.wait_ge(z_ready, s["zb"] + n - 1)
                            turn(n, r % 2, m * 2 * P)

                    def spatial():
                        pe.wait_ge(ws_masked, 1)
                        for n in range(TOKS * GROUPS // 2):
                            t, g2 = divmod(n, GROUPS // 2)
                            if g2 == 0:
                                pe.wait_ge(v_normed, 4 * TOKS + t + 1)
                            if n >= 2:
                                pe.wait_ge(sp_read, n - 1)
                            for g in (2 * g2, 2 * g2 + 1):
                                last = nc.tensor.matmul(ps[:, 6 + n % 2, (g % 2) * GD:(g % 2) * GD + GD], ws_t[:, g, :],
                                                        gm_v[:, t, g * GD:(g + 1) * GD], start=True, stop=True)
                            last.then_inc(sp_done, 1)

                    head(s, turn_ws)
                    for r in range(HEAD, R):
                        pe.wait_ge(mix_staged, s["mb"] + 2 * (r - 2) + 2)
                        if r == 6:
                            spatial()
                        for q in range(ROUND):
                            if q == 3 and r >= 6:
                                gm_turn(r - 2)
                            in_unit(ub + 4 * r + q, q, r % 2, (0, 1))
                    extra[1] = lambda: gm_turn(R - 2)
                    extra[3] = lambda: gm_turn(R - 1)

                if kind == "ffn":
                    pe.wait_ge(z_staged, 2 * (s["sb"] + R - 2) + 2)
                else:
                    pe.wait_ge(mix_staged, s["mb"] + 2 * (R - 2) + 2)
                kz = s["kz"]
                mod_at = MOD_AT[kind]
                for o in range(kz - TAIL):
                    out_unit(s, o, (0, 1))
                    if o in extra:
                        extra[o]()
                    if o == mod_at:
                        sum_mod(i + 1, s)
                for t in range(TOKS):
                    for o in range(kz - TAIL, kz):
                        out_unit(s, o, (t,))
                        if t == 0 and o == mod_at:
                            sum_mod(i + 1, s)
                        if t == 1 and o == X_TURN_AT[kind] and i + 1 < NSUBL:
                            turn_x(i + 1, 0)


_INS = ["x", "c", "ada_w", "ada_b", "norm_pre", "norm_post", "ffn_w_in", "ffn_w_out",
        "rg_w_in", "rg_conv_w", "rg_conv_b", "rg_w_a", "rg_b_a", "rg_w_x", "rg_b_x",
        "rg_lambda", "rg_w_out", "gm_w_in", "gm_ln_g", "gm_ln_b", "gm_w_s", "gm_b_s",
        "gm_w_out"]


def kernel(**inputs):
    import numpy as _np
    import concourse.bacc as _bacc
    from concourse import mybir as _mybir
    from concourse.bass_utils import run_bass_kernel_spmd as _run

    nc = _bacc.Bacc("TRN2", target_bir_lowering=False, num_devices=1)
    arrays, args = {}, []
    for name in _INS:
        a = _np.ascontiguousarray(inputs[name])
        arrays[f"in_{name}_dram"] = a
        args.append(nc.dram_tensor(f"in_{name}_dram", a.shape, _mybir.dt.from_np(a.dtype),
                                   kind="ExternalInput").ap())
    shape = arrays["in_x_dram"].shape
    args.append(nc.dram_tensor("out_0_dram", shape, _mybir.dt.float32, kind="ExternalOutput").ap())
    trunk(nc, *args)
    r = _run(nc, [arrays], core_ids=[0])
    return r.results[0]["out_0_dram"]
```
